# Optimizing a Trainium2 kernel written in Bass

```python
import jax, jax.numpy as jnp
from jax import lax
import numpy as np
import math

D_MODEL = 1024
BATCH = 1
SEQ = 512
DEPTH = 2

CHUNK = 64
N_MIXERS = 2
RET_HEADS = 4
RET_DK = D_MODEL // RET_HEADS
RET_DV = 2 * RET_DK
RET_QK = RET_HEADS * RET_DK
RET_VW = RET_HEADS * RET_DV
ROPE_BASE = 10000.0
ATT_HEADS = 16
ATT_DH = D_MODEL // ATT_HEADS
PAST_CHUNKS = 8
BAND_PAST = PAST_CHUNKS * CHUNK
BAND = (PAST_CHUNKS + 1) * CHUNK
MAX_REL = 256
REL_TABLE = MAX_REL + CHUNK
D_FF = 4 * D_MODEL
EPS = 1e-6


def _rmsnorm(x, g):
    xf = x.astype(jnp.float32)
    y = xf * lax.rsqrt(jnp.mean(xf * xf, axis=-1, keepdims=True) + EPS)
    return (y * g.astype(jnp.float32)).astype(x.dtype)

def _rope(t, pos):
    d = t.shape[-1]
    half = d // 2
    inv = jnp.exp(-jnp.log(ROPE_BASE) * jnp.arange(half, dtype=jnp.float32) / half)
    ang = pos[:, None] * inv[None, :]
    cos = jnp.cos(ang)[None, :, None, :]
    sin = jnp.sin(ang)[None, :, None, :]
    tf = t.astype(jnp.float32)
    t1, t2 = tf[..., :half], tf[..., half:]
    return jnp.concatenate([t1 * cos - t2 * sin, t1 * sin + t2 * cos], axis=-1).astype(t.dtype)

def _retention(h, w_in, gn_g, w_out):
    B, S, _ = h.shape
    nc = S // CHUNK
    proj = h @ w_in
    q, k, v, g = jnp.split(proj, [RET_QK, 2 * RET_QK, 2 * RET_QK + RET_VW], axis=-1)
    q = q.reshape(B, S, RET_HEADS, RET_DK)
    k = k.reshape(B, S, RET_HEADS, RET_DK)
    v = v.reshape(B, S, RET_HEADS, RET_DV)
    pos = jnp.arange(S, dtype=jnp.float32)
    q = _rope(q, pos)
    k = _rope(k, pos) * (RET_DK ** -0.5)

    def to_chunks(t):
        return t.reshape(B, nc, CHUNK, RET_HEADS, t.shape[-1]).transpose(1, 0, 3, 2, 4)

    qc, kc, vc = to_chunks(q), to_chunks(k), to_chunks(v)
    dt = q.dtype
    log_gamma = jnp.log1p(-jnp.exp2(-5.0 - jnp.arange(RET_HEADS, dtype=jnp.float32)))
    idx = jnp.arange(CHUNK, dtype=jnp.float32)
    intra_decay = jnp.exp(log_gamma[:, None, None] * jnp.abs(idx[:, None] - idx[None, :])).astype(dt)
    key_decay = jnp.exp(log_gamma[:, None] * (CHUNK - 1 - idx)[None, :]).astype(dt)
    query_decay = jnp.exp(log_gamma[:, None] * (idx + 1.0)[None, :]).astype(dt)
    chunk_decay = jnp.exp(log_gamma * CHUNK).astype(dt)

    def step(state, inp):
        qb, kb, vb = inp
        scores = jnp.einsum('bhid,bhjd->bhij', qb, kb) * intra_decay[None]
        o_intra = jnp.einsum('bhij,bhje->bhie', scores, vb)
        o_cross = jnp.einsum('bhid,bhde->bhie', qb, state) * query_decay[None, :, :, None]
        new_state = (state * chunk_decay[None, :, None, None]
                     + jnp.einsum('bhjd,bhje->bhde', kb * key_decay[None, :, :, None], vb))
        return new_state, o_intra + o_cross

    state0 = jnp.zeros((B, RET_HEADS, RET_DK, RET_DV), dt)
    _, o = lax.scan(step, state0, (qc, kc, vc))
    o = o.transpose(1, 0, 3, 2, 4).reshape(B, S, RET_HEADS, RET_DV).astype(jnp.float32)
    mu = jnp.mean(o, axis=-1, keepdims=True)
    var = jnp.mean(jnp.square(o - mu), axis=-1, keepdims=True)
    o = ((o - mu) * lax.rsqrt(var + EPS)).reshape(B, S, RET_VW) * gn_g.astype(jnp.float32)
    y = (jax.nn.silu(g.astype(jnp.float32)) * o).astype(h.dtype)
    return y @ w_out

def _chunk_attention(h, w_in, rel_bias, w_out):
    B, S, _ = h.shape
    nc = S // CHUNK
    q, k, v = jnp.split(h @ w_in, 3, axis=-1)
    q = q.reshape(B, S, ATT_HEADS, ATT_DH)
    k = k.reshape(B, S, ATT_HEADS, ATT_DH)
    v = v.reshape(B, S, ATT_HEADS, ATT_DH)
    pad = ((0, 0), (BAND_PAST, 0), (0, 0), (0, 0))
    kp = jnp.pad(k, pad)
    vp = jnp.pad(v, pad)
    qi = jnp.arange(CHUNK)[:, None]
    kj = jnp.arange(BAND)[None, :]
    rel = kj - BAND_PAST - qi
    bidx = jnp.maximum(rel, -MAX_REL) + MAX_REL
    bias = rel_bias[:, bidx].astype(jnp.float32)
    scale = ATT_DH ** -0.5

    def one_chunk(c):
        start = c * CHUNK
        qb = lax.dynamic_slice_in_dim(q, start, CHUNK, axis=1)
        kb = lax.dynamic_slice_in_dim(kp, start, BAND, axis=1)
        vb = lax.dynamic_slice_in_dim(vp, start, BAND, axis=1)
        s = jnp.einsum('bqhd,bkhd->bhqk', qb, kb).astype(jnp.float32) * scale + bias[None]
        valid = (start - BAND_PAST + jnp.arange(BAND)) >= 0
        s = jnp.where(valid[None, None, None, :], s, -jnp.inf)
        p = jax.nn.softmax(s, axis=-1).astype(vb.dtype)
        return jnp.einsum('bhqk,bkhd->bqhd', p, vb)

    o = lax.map(one_chunk, jnp.arange(nc))
    o = o.transpose(1, 0, 2, 3, 4).reshape(B, S, ATT_HEADS * ATT_DH)
    return o @ w_out

def _sqrelu_mlp(h, w1, w2):
    u = jax.nn.relu(h @ w1)
    return (u * u) @ w2

def first_inputs(seed: int = 0) -> dict:
    key = jax.random.key(seed)
    ks = jax.random.split(key, 12)
    n_ret = (DEPTH + 1) // 2
    n_att = DEPTH // 2
    f = jnp.float32
    x = jax.random.normal(ks[0], (BATCH, SEQ, D_MODEL), f)
    mix_norm_g = 1.0 + 0.02 * jax.random.normal(ks[1], (DEPTH, D_MODEL), f)
    ret_w_in = jax.random.normal(ks[2], (n_ret, D_MODEL, 2 * RET_QK + 2 * RET_VW), f) * D_MODEL ** -0.5
    ret_gn_g = 1.0 + 0.02 * jax.random.normal(ks[3], (n_ret, RET_VW), f)
    ret_w_out = jax.random.normal(ks[4], (n_ret, RET_VW, D_MODEL), f) * RET_VW ** -0.5
    att_w_in = jax.random.normal(ks[5], (n_att, D_MODEL, 3 * D_MODEL), f) * D_MODEL ** -0.5
    att_rel_bias = 0.1 * jax.random.normal(ks[6], (n_att, ATT_HEADS, REL_TABLE), f)
    att_w_out = jax.random.normal(ks[7], (n_att, D_MODEL, D_MODEL), f) * D_MODEL ** -0.5
    mlp_norm_g = 1.0 + 0.02 * jax.random.normal(ks[8], (DEPTH, D_MODEL), f)
    mlp_w1 = jax.random.normal(ks[9], (DEPTH, D_MODEL, D_FF), f) * D_MODEL ** -0.5
    mlp_w2 = jax.random.normal(ks[10], (DEPTH, D_FF, D_MODEL), f) * D_FF ** -0.5
    final_norm_g = 1.0 + 0.02 * jax.random.normal(ks[11], (D_MODEL,), f)
    return {"x": x, "mix_norm_g": mix_norm_g, "ret_w_in": ret_w_in, "ret_gn_g": ret_gn_g,
            "ret_w_out": ret_w_out, "att_w_in": att_w_in, "att_rel_bias": att_rel_bias,
            "att_w_out": att_w_out, "mlp_norm_g": mlp_norm_g, "mlp_w1": mlp_w1,
            "mlp_w2": mlp_w2, "final_norm_g": final_norm_g}

def first_block(x, mix_norm_g, ret_w_in, ret_gn_g, ret_w_out, att_w_in, att_rel_bias,
              att_w_out, mlp_norm_g, mlp_w1, mlp_w2, final_norm_g):
    h = x
    for i in range(DEPTH):
        hn = _rmsnorm(h, mix_norm_g[i])
        j = i // N_MIXERS
        if i % N_MIXERS == 0:
            h = h + _retention(hn, ret_w_in[j], ret_gn_g[j], ret_w_out[j])
        else:
            h = h + _chunk_attention(hn, att_w_in[j], att_rel_bias[j], att_w_out[j])
        h = h + _sqrelu_mlp(_rmsnorm(h, mlp_norm_g[i]), mlp_w1[i], mlp_w2[i])
    return _rmsnorm(h, final_norm_g)


DEPTH_2 = 1

HEAD_DIM = 64
A_HEADS = 4
B_HEADS = 4
C_HEADS = 8
C_KV_HEADS = 2
A_W = A_HEADS * HEAD_DIM
B_W = B_HEADS * HEAD_DIM
C_QW = C_HEADS * HEAD_DIM
C_KVW = C_KV_HEADS * HEAD_DIM
N_BRANCH = 3
IN_SIZES = (A_W, A_W, A_W, B_W, B_W, B_W, B_HEADS, C_QW, C_KVW, C_KVW, D_MODEL, D_MODEL, D_MODEL)
IN_COLS = sum(IN_SIZES)
MOBA_BLOCK = 256
MOBA_TOPK = 3
Q_BLOCK = 128
WINDOW = 128
NUM_BUCKETS = 32
MAX_DISTANCE = 4096
D_FF_2 = 2816
CONV_WIDTH = 3
NEG = -1e30
SCALE = HEAD_DIM ** -0.5


def rmsnorm(x, g):
    xf = x.astype(jnp.float32)
    y = xf * lax.rsqrt(jnp.mean(xf * xf, axis=-1, keepdims=True) + EPS)
    return (y * g.astype(jnp.float32)).astype(x.dtype)

def t5_bucket(dist):
    dist = jnp.maximum(dist, 0)
    max_exact = NUM_BUCKETS // 2
    d = jnp.maximum(dist.astype(jnp.float32), 1.0)
    large = max_exact + (jnp.log(d / max_exact) / math.log(MAX_DISTANCE / max_exact)
                         * (NUM_BUCKETS - max_exact)).astype(jnp.int32)
    large = jnp.minimum(large, NUM_BUCKETS - 1)
    return jnp.where(dist < max_exact, dist, large)

def moba_attention(q, k, v, tbl):
    Bn, S, H, Dh = q.shape
    s_pad = -(-S // MOBA_BLOCK) * MOBA_BLOCK
    nb = s_pad // MOBA_BLOCK
    ksel = min(MOBA_TOPK, nb)
    qt = q.transpose(0, 2, 1, 3)
    pad = ((0, 0), (0, 0), (0, s_pad - S), (0, 0))
    k_blocks = jnp.pad(k.transpose(0, 2, 1, 3), pad).reshape(Bn, H, nb, MOBA_BLOCK, Dh)
    v_blocks = jnp.pad(v.transpose(0, 2, 1, 3), pad).reshape(Bn, H, nb, MOBA_BLOCK, Dh)
    k_mean = jnp.mean(k_blocks.astype(jnp.float32), axis=3)
    gate = jnp.einsum('bhsd,bhnd->bhsn', qt.astype(jnp.float32), k_mean)
    q_blk = jnp.arange(S) // MOBA_BLOCK
    past = jnp.arange(nb)[None, :] < q_blk[:, None]
    gate = jnp.where(past, gate, -jnp.inf)
    _, sel = lax.top_k(gate, ksel)
    valid = sel < q_blk[:, None]
    nq = S // Q_BLOCK
    qc = qt.reshape(Bn, H, nq, Q_BLOCK, Dh).transpose(2, 0, 1, 3, 4)
    selc = sel.reshape(Bn, H, nq, Q_BLOCK, ksel).transpose(2, 0, 1, 3, 4)
    validc = valid.reshape(Bn, H, nq, Q_BLOCK, ksel).transpose(2, 0, 1, 3, 4)
    bi = jnp.arange(Bn)[:, None, None, None]
    hi = jnp.arange(H)[None, :, None, None]
    blk_ar = jnp.arange(MOBA_BLOCK)

    def chunk(args):
        c, qb, sb, vb = args
        t = c * Q_BLOCK + jnp.arange(Q_BLOCK)
        kg = k_blocks[bi, hi, sb].reshape(Bn, H, Q_BLOCK, ksel * MOBA_BLOCK, Dh)
        vg = v_blocks[bi, hi, sb].reshape(Bn, H, Q_BLOCK, ksel * MOBA_BLOCK, Dh)
        s_pos = (sb[..., None] * MOBA_BLOCK + blk_ar).reshape(Bn, H, Q_BLOCK, ksel * MOBA_BLOCK)
        lg = jnp.einsum('bhqd,bhqkd->bhqk', qb, kg).astype(jnp.float32) * SCALE
        lg = lg + tbl[hi, t5_bucket(t[:, None] - s_pos)].astype(jnp.float32)
        lg = jnp.where(jnp.repeat(vb, MOBA_BLOCK, axis=-1), lg, NEG)
        own = (c * Q_BLOCK) // MOBA_BLOCK
        ko = lax.dynamic_index_in_dim(k_blocks, own, axis=2, keepdims=False)
        vo = lax.dynamic_index_in_dim(v_blocks, own, axis=2, keepdims=False)
        dist = t[:, None] - (own * MOBA_BLOCK + blk_ar)[None, :]
        lo = jnp.einsum('bhqd,bhkd->bhqk', qb, ko).astype(jnp.float32) * SCALE
        lo = lo + tbl[:, t5_bucket(dist)].astype(jnp.float32)
        lo = jnp.where(dist >= 0, lo, NEG)
        p = jax.nn.softmax(jnp.concatenate([lg, lo], axis=-1), axis=-1)
        pg = p[..., :ksel * MOBA_BLOCK].astype(v.dtype)
        po = p[..., ksel * MOBA_BLOCK:].astype(v.dtype)
        return (jnp.einsum('bhqk,bhqkd->bhqd', pg, vg)
                + jnp.einsum('bhqk,bhkd->bhqd', po, vo))

    out = lax.map(chunk, (jnp.arange(nq), qc, selc, validc))
    return out.transpose(1, 0, 3, 2, 4).reshape(Bn, S, H * Dh)

def forgetting_attention(q, k, v, f_logit):
    Bn, S, H, Dh = q.shape
    logf = jax.nn.log_sigmoid(f_logit.astype(jnp.float32))
    cum = jnp.cumsum(logf, axis=1).transpose(0, 2, 1)
    kt = k.transpose(0, 2, 1, 3)
    vt = v.transpose(0, 2, 1, 3)
    nq = S // Q_BLOCK
    qc = q.transpose(0, 2, 1, 3).reshape(Bn, H, nq, Q_BLOCK, Dh).transpose(2, 0, 1, 3, 4)
    cc = cum.reshape(Bn, H, nq, Q_BLOCK).transpose(2, 0, 1, 3)
    s_pos = jnp.arange(S)

    def block(args):
        i, qb, cb = args
        t = i * Q_BLOCK + jnp.arange(Q_BLOCK)
        lg = jnp.einsum('bhqd,bhkd->bhqk', qb, kt).astype(jnp.float32) * SCALE
        lg = lg + cb[..., None] - cum[:, :, None, :]
        lg = jnp.where(s_pos[None, :] <= t[:, None], lg, NEG)
        p = jax.nn.softmax(lg, axis=-1).astype(vt.dtype)
        return jnp.einsum('bhqk,bhkd->bhqd', p, vt)

    out = lax.map(block, (jnp.arange(nq), qc, cc))
    return out.transpose(1, 0, 3, 2, 4).reshape(Bn, S, H * Dh)

def sliding_window_sink_attention(q, k, v, sinks, tbl):
    Bn, S, Hq, Dh = q.shape
    Hkv = k.shape[2]
    G = Hq // Hkv
    nq = S // Q_BLOCK
    qb = q.reshape(Bn, nq, Q_BLOCK, Hkv, G, Dh)
    kb = k.reshape(Bn, nq, Q_BLOCK, Hkv, Dh)
    vb = v.reshape(Bn, nq, Q_BLOCK, Hkv, Dh)
    shift = ((0, 0), (1, 0), (0, 0), (0, 0), (0, 0))
    kband = jnp.concatenate([jnp.pad(kb, shift)[:, :-1], kb], axis=2)
    vband = jnp.concatenate([jnp.pad(vb, shift)[:, :-1], vb], axis=2)
    lg = jnp.einsum('bnqhgd,bnkhd->bnhgqk', qb, kband).astype(jnp.float32) * SCALE
    tl = jnp.arange(Q_BLOCK)
    sl = jnp.arange(2 * Q_BLOCK)
    dist = tl[:, None] + Q_BLOCK - sl[None, :]
    key_pos = (jnp.arange(nq)[:, None] - 1) * Q_BLOCK + sl[None, :]
    mask = ((dist >= 0) & (dist < WINDOW))[None] & (key_pos >= 0)[:, None, :]
    bias = tbl[:, t5_bucket(dist)].astype(jnp.float32).reshape(Hkv, G, Q_BLOCK, 2 * Q_BLOCK)
    lg = jnp.where(mask[None, :, None, None], lg + bias, NEG)
    sink = jnp.broadcast_to(sinks.astype(jnp.float32).reshape(Hkv, G)[:, :, None, None],
                            lg.shape[:-1] + (1,))
    p = jax.nn.softmax(jnp.concatenate([lg, sink], axis=-1), axis=-1)[..., :-1]
    out = jnp.einsum('bnhgqk,bnkhd->bnqhgd', p.astype(v.dtype), vband)
    return out.reshape(Bn, S, Hq * Dh)

def causal_dwconv(u, w, b):
    C = u.shape[-1]
    y = lax.conv_general_dilated(u, w[:, None, :].astype(u.dtype), window_strides=(1,),
                                 padding=[(CONV_WIDTH - 1, 0)],
                                 dimension_numbers=('NWC', 'WIO', 'NWC'),
                                 feature_group_count=C)
    return y + b

def hybrid_layer(x, ln1, w_in, b_f, sinks, w_pa, w_pb, w_pc, w_o, ln2, w_up, conv_w, conv_b,
                 w_down, tbl_a, tbl_c):
    Bn, S, _ = x.shape
    h = rmsnorm(x, ln1)
    z = h @ w_in
    points = np.cumsum(IN_SIZES)[:-1].tolist()
    qa, ka, va, qb, kb, vb, fb, qc, kc, vc, ga, gb, gc = jnp.split(z, points, axis=-1)

    def heads(t, n):
        return t.reshape(Bn, S, n, HEAD_DIM)

    o_a = moba_attention(heads(qa, A_HEADS), heads(ka, A_HEADS), heads(va, A_HEADS), tbl_a)
    o_b = forgetting_attention(heads(qb, B_HEADS), heads(kb, B_HEADS), heads(vb, B_HEADS), fb + b_f)
    o_c = sliding_window_sink_attention(heads(qc, C_HEADS), heads(kc, C_KV_HEADS),
                                        heads(vc, C_KV_HEADS), sinks, tbl_c)
    merged = (jax.nn.sigmoid(ga) * (o_a @ w_pa)
              + jax.nn.sigmoid(gb) * (o_b @ w_pb)
              + jax.nn.sigmoid(gc) * (o_c @ w_pc))
    x = x + merged @ w_o

    h2 = rmsnorm(x, ln2)
    u = causal_dwconv(h2 @ w_up, conv_w, conv_b)
    a, b = jnp.split(u, 2, axis=-1)
    return x + (jax.nn.silu(a) * b) @ w_down

def second_inputs(seed: int = 0) -> dict:
    key = jax.random.key(seed)
    ks = jax.random.split(key, 16)

    def nrm(k, shape, scale):
        return jax.random.normal(k, shape, jnp.float32) * scale

    return {
        "x": nrm(ks[0], (BATCH, SEQ, D_MODEL), 1.0),
        "ln1": 1.0 + nrm(ks[1], (DEPTH_2, D_MODEL), 0.05),
        "w_in": nrm(ks[2], (DEPTH_2, D_MODEL, IN_COLS), D_MODEL ** -0.5),
        "b_f": 4.0 + nrm(ks[3], (DEPTH_2, B_HEADS), 0.5),
        "sinks": nrm(ks[4], (DEPTH_2, C_HEADS), 1.0),
        "w_pa": nrm(ks[5], (DEPTH_2, A_W, D_MODEL), A_W ** -0.5),
        "w_pb": nrm(ks[6], (DEPTH_2, B_W, D_MODEL), B_W ** -0.5),
        "w_pc": nrm(ks[7], (DEPTH_2, C_QW, D_MODEL), C_QW ** -0.5),
        "w_o": nrm(ks[8], (DEPTH_2, D_MODEL, D_MODEL), D_MODEL ** -0.5),
        "ln2": 1.0 + nrm(ks[9], (DEPTH_2, D_MODEL), 0.05),
        "w_up": nrm(ks[10], (DEPTH_2, D_MODEL, 2 * D_FF_2), D_MODEL ** -0.5),
        "conv_w": nrm(ks[11], (DEPTH_2, CONV_WIDTH, 2 * D_FF_2), CONV_WIDTH ** -0.5),
        "conv_b": nrm(ks[12], (DEPTH_2, 2 * D_FF_2), 0.02),
        "w_down": nrm(ks[13], (DEPTH_2, D_FF_2, D_MODEL), D_FF_2 ** -0.5),
        "rel_bias": nrm(ks[14], (NUM_BUCKETS, A_HEADS + C_HEADS), 0.5),
        "ln_f": 1.0 + nrm(ks[15], (D_MODEL,), 0.05),
    }

def second_block(x, ln1, w_in, b_f, sinks, w_pa, w_pb, w_pc, w_o, ln2, w_up, conv_w, conv_b,
              w_down, rel_bias, ln_f):
    tbl_a = rel_bias[:, :A_HEADS].T
    tbl_c = rel_bias[:, A_HEADS:].T
    for l in range(DEPTH_2):
        x = hybrid_layer(x, ln1[l], w_in[l], b_f[l], sinks[l], w_pa[l], w_pb[l], w_pc[l], w_o[l],
                         ln2[l], w_up[l], conv_w[l], conv_b[l], w_down[l], tbl_a, tbl_c)
    return rmsnorm(x, ln_f)


def setup_inputs(seed=0):
    out = dict(first_inputs(seed))
    for name, value in second_inputs(seed + 1).items():
        if name != "x":
            out[name + "_2"] = value
    return out


def reference(
    x, mix_norm_g, ret_w_in, ret_gn_g, ret_w_out, att_w_in, att_rel_bias, att_w_out, mlp_norm_g,
    mlp_w1, mlp_w2, final_norm_g, ln1_2, w_in_2, b_f_2, sinks_2, w_pa_2, w_pb_2, w_pc_2, w_o_2,
    ln2_2, w_up_2, conv_w_2, conv_b_2, w_down_2, rel_bias_2, ln_f_2,
):
    x = first_block(
        x, mix_norm_g, ret_w_in, ret_gn_g, ret_w_out, att_w_in, att_rel_bias, att_w_out,
        mlp_norm_g, mlp_w1, mlp_w2, final_norm_g,
    )
    return second_block(
        x, ln1_2, w_in_2, b_f_2, sinks_2, w_pa_2, w_pb_2, w_pc_2, w_o_2, ln2_2, w_up_2,
        conv_w_2, conv_b_2, w_down_2, rel_bias_2, ln_f_2,
    )


_drawn_inputs = setup_inputs


def setup_inputs(seed=0):
    import zlib

    import numpy as np

    out = dict(_drawn_inputs(seed))
    spreads = {}
    factors = {'ret_gn_g': 4.621,
     'att_rel_bias': 23.024,
     'b_f_2': 22.136,
     'sinks_2': 7.701,
     'conv_b_2': 4.025,
     'mlp_norm_g': 4.037,
     'ln1_2': 3.106,
     'ln2_2': 3.851}
    for name, (base, spread) in spreads.items():
        noise = np.random.default_rng([zlib.crc32(name.encode()), seed]).standard_normal(out[name].shape)
        drawn = base * np.exp(spread * noise) if base else spread * noise
        out[name] = __import__('jax').numpy.asarray(drawn.astype(out[name].dtype))
    for name, factor in factors.items():
        out[name] = (out[name] * factor).astype(out[name].dtype)
    return out
```

```python
from contextlib import ExitStack

import numpy as np
import concourse.bass as bass
from concourse import mybir

F32 = mybir.dt.float32
F32R = mybir.dt.float32r
ALU = mybir.AluOpType
ACT = mybir.ActivationFunctionType

P = 128
S = 512
D = 1024
KT = D // P
TT = S // P
EPS = 1e-6
NEG = -1e30
LOWEST = -3.4028235e38
UNIT = 1024
RING = 4
LEAD = 3

RH, RK, RV, CH = 4, 256, 512, 64
AH = 16
REL_MAX, REL_TABLE = 256, 320
BUCKETS, MAX_DISTANCE = 32, 4096
HEAD = 64
FF2 = 2816
PAIRS = FF2 // P
GROUPS = [6, 6, 6, 4]
SCALE = HEAD ** -0.5
STRIP = 640

C_MIX0, C_MLP0, C_MIX1, C_MLP1, C_FIN, C_LN1, C_LN2, C_LNF = [8 * n for n in range(8)]
C_GN = 64
C_CW = C_GN + RH * RV // P
C_CB = C_CW + 3 * 2 * PAIRS
N_COLS = C_CB + 2 * PAIRS

U_RET = 12 + 3 * 16 + 4
U_MLP = 64
U_ATT = 8 + 16 + 8
U_HEADS = 5 + 13
U_MERGE = 4 * KT
U_WO = KT
U_GLU = 2 * PAIRS + len(GROUPS) * KT
N_UNITS = U_RET + U_MLP + U_ATT + U_MLP + U_HEADS + U_MERGE + U_WO + U_GLU

P_AT, P_W = [0, 128, 384, 768], [128, 256, 384, 512]
T_AT, T_W = [0, 512, 896, 1152], [512, 384, 256, 128]
CP_AT, CP_W = [0, 128, 384, 640], [128, 256, 256, 256]
CT_AT, CT_W = [0, 256, 512, 768], [256, 256, 256, 128]


HYB_UNITS = {-1: (2, (1, 0)), 0: (3, (1, 1)), 1: (4, (0, 0)), 2: (5, (0, 1)), 3: (6, (1, 0)), 4: (7, (1, 1)),
             5: (8, (0, 0)), 6: (9, (0, 1)), 7: (10, (1, 0)), 9: (11, (0, 0)), 11: (12, (1, 0))}
HYB_TILES = [2, 4, 6, 8, 10, 11, 12, 13]
SINK_OF = [j + 4 * half for j in range(4) for half in range(2)]
BIAS_COUNT = [16, 16, 32, 32, None, None, None, None] + [48 + 16 * (n // 2) for n in range(8)]


class Lin:

    def __init__(self, b, a=0, i=None):
        self.b, self.a, self.i = b, a, i

    def __add__(self, n):
        return Lin(self.b + n, self.a, self.i)

    def __sub__(self, n):
        return self + -n

    def __mul__(self, n):
        return Lin(self.b * n, self.a * n, self.i)

    def __floordiv__(self, n):
        assert self.a % n == 0
        return Lin(self.b // n, self.a // n, self.i)

    def __mod__(self, n):
        assert self.a % n == 0
        return self.b % n

    def val(self):
        if not self.a or self.i is None:
            return self.b
        x = self.i if self.a == 1 else self.i * self.a
        return x + self.b if self.b else x

    def fold(self, m):
        return Lin(self.b % m, self.a, self.i)

    def positive(self):
        return self.b > 0 or bool(self.a)


def lin(x):
    return x if isinstance(x, Lin) else Lin(x)


def holder(sem):
    k = [0]

    def hold(eng, *waits):
        counts = [lin(count).val() for _, count in waits]
        counts = [c if isinstance(c, int) else eng.to_reg(c) for c in counts]
        if any(not isinstance(c, int) for c in counts):
            k[0] = k[0] % 16 + 1
            eng.wait_ge(sem, k[0])
        for (of, count), c in zip(waits, counts):
            assert lin(count).b > 0 or not lin(count).a
            if lin(count).positive():
                eng.wait_ge(of, c)
    return hold


class Place:

    def __init__(self):
        self.u, self.pe, self.t = Lin(0), Lin(0), Lin(0)

    def enter(self, i, du, dpe, dt):
        self.start = [self.u.b, self.pe.b, self.t.b]
        self.per = [du, dpe, dt]
        self.u, self.pe, self.t = (Lin(b, a, i) for b, a in zip(self.start, self.per))

    def leave(self, n):
        now = [self.u.b, self.pe.b, self.t.b]
        assert now == [b + a for b, a in zip(self.start, self.per)], (now, self.start, self.per)
        self.u, self.pe, self.t = (Lin(b + n * a) for b, a in zip(self.start, self.per))

    def step(self, pe=1, t=1):
        self.u, self.pe, self.t = self.u + 1, self.pe + pe, self.t + t


def wait(eng, sem, count):
    count = lin(count)
    assert count.b > 0 or not count.a, count.b
    if count.positive():
        eng.wait_ge(sem, count.val())


def build(nc, stream, x_t, cols, wf, f_bias, sinks, rel_pad, rel_2, c_rope, c_decay, c_sq, c_tri, c_sel,
          c_onehot, out):
    strips = nc.dram_tensor("bias_strips", (12, P, STRIP), F32, kind="Internal").ap()
    with ExitStack() as ctx:
        def sb(name, shape, dt=F32):
            return ctx.enter_context(nc.sbuf_tensor(name, shape, dt))

        def sem(name):
            return ctx.enter_context(nc.semaphore(name))

        raw = sb("raw", [P, RING, UNIT])
        w_hi = sb("w_hi", [P, RING, UNIT], F32R)
        w_lo = sb("w_lo", [P, RING, UNIT], F32R)
        h = sb("h", [P, KT, S])
        x_hi = sb("x_hi", [P, KT, S], F32R)
        x_lo = sb("x_lo", [P, KT, S], F32R)
        rbc = sb("rbc", [P, S])
        sq = sb("sq", [P, 4, S])
        acc = sb("acc", [P, S])
        diag = sb("diag", [P, TT, P])
        ident = sb("ident", [P, P])
        ones = sb("ones", [P, P])
        sqr = sb("sqr", [P, 4, P], F32R)
        colv = sb("colv", [P, N_COLS])
        small = sb("small", [P, 12, 16])
        wf_raw = sb("wf_raw", [P, KT, 4])
        wf_hi = sb("wf_hi", [P, KT, 4], F32R)
        wf_lo = sb("wf_lo", [P, KT, 4], F32R)
        rel_sb = sb("rel_sb", [BUCKETS, 12])
        arena = sb("arena", [P, 17 * S])
        arena_r = sb("arena_r", [P, 29 * S], F32R)

        banks = [ctx.enter_context(nc.psum_tensor(f"bank{n}", [P, S], F32)) for n in range(8)]

        def f_at(tile, n=1):
            return arena[:, tile * S:(tile + n) * S]

        def r_at(tile, n=1):
            return arena_r[:, tile * S:(tile + n) * S]

        def f32(ap):
            return ap.bitcast(F32)

        def col(n):
            n = lin(n)
            return colv[:, n.b:n.b + 1] if not n.a else colv[:, bass.ds(n.val(), 1)]

        ms, sd, rcol = small[:, 0, 0:4], small[:, 1, 0:4], small[:, 2, 0:4]
        gn_ms, gn_sd, gn_r = small[:, 0, 4:8], small[:, 1, 4:8], small[:, 2, 4:8]
        mx = [small[:, 3, 4 * n:4 * n + 4] for n in range(2)]
        nm = [small[:, 4, 4 * n:4 * n + 4] for n in range(2)]
        sums = [small[:, 5, 4 * n:4 * n + 4] for n in range(2)]
        rinv = [small[:, 6, 4 * n:4 * n + 4] for n in range(2)]
        es = [small[:, 3, 8 + 4 * n:12 + 4 * n] for n in range(2)]
        sink_b, nsink = small[:, 7, 0:8], small[:, 7, 8:16]
        fb_b = small[:, 6, 8:12]
        fl, fe, fn = small[:, 8, :], small[:, 9, :], small[:, 10, :]
        flog = small[:, 11, :]
        sums2 = [small[:, 4, 8 + 4 * n:12 + 4 * n] for n in range(2)]

        x_landed = [sem(f"x_landed{j}") for j in range(KT)]
        cols_landed = sem("cols_landed")
        squares_landed = sem("squares_landed")
        masks_landed = sem("masks_landed")
        masks_ready = sem("masks_ready")
        rope_landed = sem("rope_landed")
        strip_in = sem("strip_in")
        small_in = sem("small_in")
        strip_made = sem("strip_made")
        strip_copied = sem("strip_copied")
        strip_saved = sem("strip_saved")
        consts_made = sem("consts_made")
        raw_landed = [sem(f"raw_landed{n}") for n in range(RING)]
        hi_ready = sem("hi_ready")
        lo_ready = sem("lo_ready")
        products_done = sem("products_done")
        tile_read = sem("tile_read")
        xh_ready = sem("xh_ready")
        xl_ready = sem("xl_ready")
        sq_ready = sem("sq_ready")
        acc_sum = sem("acc_sum")
        stat_done = sem("stat_done")
        ms_ready = sem("ms_ready")
        sd_ready = sem("sd_ready")
        rcol_ready = sem("rcol_ready")
        diag_ready = sem("diag_ready")
        rbc_ready = sem("rbc_ready")
        hn_ready = sem("hn_ready")
        rope_tables = sem("rope_tables")
        rope_ready = sem("rope_ready")
        rope_hi = sem("rope_hi")
        rope_lo = sem("rope_lo")
        v_hi = sem("v_hi")
        v_lo = sem("v_lo")
        decay_landed = sem("decay_landed")
        ret_scores = sem("ret_scores")
        ret_p = sem("ret_p")
        ret_p_hi = sem("ret_p_hi")
        ret_p_lo = sem("ret_p_lo")
        ret_pv = sem("ret_pv")
        ret_o = sem("ret_o")
        gn_sum = sem("gn_sum")
        gn_done = sem("gn_done")
        gn_centred = sem("gn_centred")
        gn_sq = sem("gn_sq")
        gn_ms_r = sem("gn_ms_r")
        gn_sd_r = sem("gn_sd_r")
        gn_r_r = sem("gn_r_r")
        gn_diag = sem("gn_diag")
        gate_ready = sem("gate_ready")
        y_scaled = sem("y_scaled")
        y_ready = sem("y_ready")
        y_hi = sem("y_hi")
        y_lo = sem("y_lo")
        u_ready = sem("u_ready")
        u_hi = sem("u_hi")
        u_lo = sem("u_lo")

        class Heads:

            def __init__(self, n):
                self.scores = sem(f"{n}_scores")
                self.biased = sem(f"{n}_biased")
                self.negmax = sem(f"{n}_negmax")
                self.exp = sem(f"{n}_exp")
                self.rinv = sem(f"{n}_rinv")
                self.probs = sem(f"{n}_probs")
                self.turned = sem(f"{n}_turned")
                self.turned_hi = sem(f"{n}_turned_hi")
                self.turned_lo = sem(f"{n}_turned_lo")
                self.pv = sem(f"{n}_pv")
                self.o = sem(f"{n}_o")
                self.qk_hi = sem(f"{n}_qk_hi")
                self.qk_lo = sem(f"{n}_qk_lo")
                self.bias = [sem(f"{n}_bias0"), sem(f"{n}_bias1")]

        att = Heads("att")
        hyb = Heads("hyb")
        att_v = sem("att_v")
        stage_hi = sem("stage_hi")
        stage_lo = sem("stage_lo")
        hyb_vh = sem("hyb_vh")
        hyb_vl = sem("hyb_vl")
        wf_h = sem("wf_h")
        wf_l = sem("wf_l")
        tri_landed = sem("tri_landed")
        f_done = sem("f_done")
        f_row_ready = sem("f_row_ready")
        f_step = sem("f_step")
        f_act = sem("f_act")
        cum_done = sem("cum_done")
        cum_row = sem("cum_row")
        cum_bc = sem("cum_bc")
        cum_bias = sem("cum_bias")
        sink_ready = sem("sink_ready")
        sink_exp = sem("sink_exp")
        sink_sum = sem("sink_sum")
        o_hi = sem("o_hi")
        o_lo = sem("o_lo")
        gate_read = sem("gate_read")
        gate_sig = sem("gate_sig")
        branch_read = sem("branch_read")
        merge_a = sem("merge_a")
        merged = sem("merged")
        pad_made = sem("pad_made")
        conv_0 = sem("conv_0")
        conv_1 = sem("conv_1")
        conv_2 = sem("conv_2")
        silu_done = sem("silu_done")
        s_ready = sem("s_ready")
        s_hi = sem("s_hi")
        s_lo = sem("s_lo")
        out_ready = sem("out_ready")
        stored = sem("stored")

        cosr, sinr = f_at(0), f_at(1)
        rt = [f_at(2 + n) for n in range(4)]
        qkf = [f_at(6), f_at(7)]
        pf_ret = f_at(2, 3)
        oc = [f_at(8 + n) for n in range(4)]
        sg = [f_at(12 + n) for n in range(4)]
        decay = f_at(16)
        rqk_h = [r_at(n) for n in range(4)]
        rqk_l = [r_at(4 + n) for n in range(4)]
        rv_h = [r_at(8 + n) for n in range(4)]
        rv_l = [r_at(12 + n) for n in range(4)]
        rp_h, rp_l = arena_r[:, 16 * S:16 * S + 1280], arena_r[:, 16 * S + 1280:16 * S + 2560]
        ry_h = [r_at(21 + n) for n in range(4)]
        ry_l = [r_at(25 + n) for n in range(4)]
        onehot_sb = arena[0:BUCKETS, 8 * S:8 * S + STRIP]
        strip_sb = arena[0:12, 10 * S:10 * S + STRIP]
        masks_sb = f_at(12).rearrange("p (m n) -> p m n", m=4)
        zf = [f_at(0), f_at(1)]
        uf = [f_at(2), f_at(3)]
        uh = [r_at(n) for n in range(KT)]
        ul = [r_at(8 + n) for n in range(KT)]
        pf = [arena[:, n * 1280:(n + 1) * 1280] for n in range(2)]
        af = [f_at(5), f_at(6)]
        bias = [f_at(7), f_at(8)]
        vf = arena[:, 9 * S:17 * S].rearrange("p (a t d) -> p a t d", a=8, t=TT)
        of = [f_at(9 + n) for n in range(KT)]

        def pair_tile(pair, a=0, b=P):
            if not pair.a:
                return arena[a:b, (9 + pair.b) * S:(10 + pair.b) * S]
            return arena[a:b, bass.ds((pair * S + 9 * S).val(), S)]

        def mf_at(c):
            return mf[:, c.b, :] if not c.a else arena[:, bass.ds((c * S + 9 * S).val(), S)]

        ah = [[r_at(2 * n + m) for m in range(2)] for n in range(2)]
        al = [[r_at(4 + 2 * n + m) for m in range(2)] for n in range(2)]
        pt_h, pt_l = arena_r[:, 8 * S:8 * S + 1280], arena_r[:, 8 * S + 1280:8 * S + 2560]
        vs_h, vs_l = r_at(13), r_at(14)
        ao_h = [r_at(15 + n) for n in range(KT)]
        ao_l = [r_at(23 + n) for n in range(6)] + [r_at(n) for n in range(2)]
        hv_h = [r_at(13 + n) for n in range(4)]
        hv_l = [r_at(17 + n) for n in range(4)]
        hc_h, hc_l = r_at(21), r_at(22)
        f_row = arena[0:4, 13 * S:14 * S]
        tri_sb, cum_sb, sel_sb = f_at(16), arena[0:4, 15 * S:16 * S], arena[0:4, 14 * S:15 * S]
        oh = [r_at(n) for n in range(KT)]
        ol = [r_at(8 + n) for n in range(KT)]
        gf = [f_at(n) for n in range(3)]
        mt = [f_at(3 + n) for n in range(4)]
        mf = arena[:, 9 * S:17 * S].rearrange("p (c n) -> p c n", c=KT)
        mg_h = [r_at(16 + n) for n in range(KT)]
        mg_l = [r_at(24 + n) for n in range(5)] + [r_at(n) for n in range(3)]
        cz = [arena[:, n * 520:n * 520 + S + 2] for n in range(4)]
        cy = [f_at(5 + n) for n in range(4)]
        sf = [f_at(9), f_at(10)]
        sh_all = arena_r[:, 0:12 * S].rearrange("p (c n) -> p c n", c=12)
        sl_all = arena_r[:, 12 * S:24 * S].rearrange("p (c n) -> p c n", c=12)

        block = ctx.enter_context(nc.Block())

        @block.sync
        def _(sp):
            flat = stream.rearrange("u p n -> (u p) n")
            for u in range(RING):
                sp.dma_start(raw[:, u, :], flat[u * P:(u + 1) * P, :]).then_inc(raw_landed[u], 16)
            with sp.Fori(0, N_UNITS // RING - 1) as i:
                for j in range(RING):
                    u = Lin(RING + j, RING, i)
                    wait(sp, lo_ready, u - (RING - 1))
                    sp.dma_start(raw[:, j, :], flat[bass.ds((u * P).val(), P), :]).then_inc(raw_landed[j], 16)
            for u in range(N_UNITS // RING * RING, N_UNITS):
                wait(sp, lo_ready, u - (RING - 1))
                sp.dma_start(raw[:, u % RING, :], flat[u * P:(u + 1) * P, :]).then_inc(raw_landed[u % RING], 16)
            for j in range(KT):
                wait(sp, out_ready, j + 1)
                sp.dma_start(out[j * P:(j + 1) * P, :], h[:, j, :]).then_inc(stored, 16)
            sp.wait_ge(stored, 16 * KT)

        @block.tensor
        def _(pe):
            at = Place()

            def mm3(dst, left, right, start, stop, check=True):
                (lh, ll), (rh, rl) = left, right
                kw = {} if check else {"skip_group_check": True}
                pe.matmul(dst, lh, rh, start=start, stop=False, **kw)
                pe.matmul(dst, lh, rl, start=False, stop=False, **kw)
                return pe.matmul(dst, ll, rh, start=False, stop=stop, **kw)

            def xs(k):
                return x_hi[:, k, :], x_lo[:, k, :]

            def w_at(slot, a, b):
                return w_hi[:, slot, a:b], w_lo[:, slot, a:b]

            def proj(src=xs, n=KT, first=None, hooks={}, bank=None):
                slot = at.u % RING
                wait(pe, lo_ready, at.u + 1)
                rotating = bank is None
                if rotating:
                    bank = banks[at.t % 2]
                    wait(pe, tile_read, at.t - 1)
                for k in range(n):
                    if k in hooks:
                        hooks[k]()
                    if first:
                        for s, base in first:
                            wait(pe, s, lin(base) + (k + 1))
                    m = mm3(bank[:, :], w_at(slot, k * P, k * P + P), src(k), k == 0, k == n - 1)
                m.then_inc(products_done, 1)
                at.step(1, 1 if rotating else 0)

            def token_major(kk, first=None, hooks={}):
                slot = at.u % RING
                wait(pe, lo_ready, at.u + 1)
                for k in range(2):
                    if k in hooks:
                        hooks[k]()
                    for t in range(TT):
                        xk = (x_hi[:, 2 * kk + k, t * P:t * P + P], x_lo[:, 2 * kk + k, t * P:t * P + P])
                        m = mm3(banks[4 + t][:, :], xk, w_at(slot, k * S, k * S + S),
                                kk == 0 and k == 0, kk == 3 and k == 1)
                m.then_inc(products_done, 1)
                at.step(1, 0)

            def mean_square(n):
                wait(pe, acc_sum, 6 * (n + 1))
                wait(pe, sq_ready, 8 * (n + 1))
                wait(pe, consts_made, 1)
                for t in range(TT):
                    pe.matmul(banks[2][:, t:t + 1], acc[:, t * P:t * P + P], ones[:, 0:1], start=True, stop=False)
                    m = pe.matmul(banks[2][:, t:t + 1], sq[:, 3, t * P:t * P + P], ones[:, 0:1],
                                  start=False, stop=True)
                m.then_inc(stat_done, 1)

            def spread_rms(n):
                wait(pe, diag_ready, n + 1)
                pe.matmul(banks[3][:, :], ones[:, :], diag[:, :, :], start=True, stop=True).then_inc(stat_done, 1)

            pe.wait_ge(strip_in, 32)
            pe.matmul(banks[6][0:12, 0:512], rel_sb[:, :], onehot_sb[:, 0:512], start=True, stop=True)
            pe.matmul(banks[7][0:12, 0:128], rel_sb[:, :], onehot_sb[:, 512:640], start=True, stop=True)\
                .then_inc(strip_made, 1)

            def gn_spread(hd):
                wait(pe, gn_diag, hd + 1)
                pe.matmul(banks[2][:, :], ones[:, :], diag[:, :, :], start=True, stop=True).then_inc(gn_done, 1)

            def ret_out():
                for _ in range(4):
                    slot = at.u % RING
                    wait(pe, lo_ready, at.u + 1)
                    for c in range(2):
                        wait(pe, tile_read, at.t - 1)
                        for k in range(4):
                            m = mm3(banks[at.t % 2][:, :], w_at(slot, (4 * c + k) * P, (4 * c + k + 1) * P),
                                    (ry_h[k], ry_l[k]), k == 0, k == 3)
                        m.then_inc(products_done, 1)
                        at.pe, at.t = at.pe + 1, at.t + 1
                    at.u = at.u + 1

            def ret_head(hd, first):
                if first:
                    proj(first=[(xl_ready, 0)], hooks={7: lambda: mean_square(0)})
                    proj(hooks={4: lambda: spread_rms(0)})
                else:
                    proj(hooks={5: lambda: gn_spread(hd - 1)})
                    proj()
                proj()
                proj()
                if first:
                    pe.wait_ge(strip_copied, 1)
                wait(pe, ret_o, hd * 4)
                for kk in range(4):
                    token_major(kk)
                if not first:
                    wait(pe, y_lo, hd * 4)
                    ret_out()
                wait(pe, rope_lo, hd * 4 + 4)
                for j, (b, o) in enumerate([(2, 0), (3, 0), (4, 0), (4, 256)]):
                    if j == 2:
                        wait(pe, v_lo, hd * 4 + 4)
                    for d in range(2):
                        keys = (rqk_h[2 + d][:, j * P:j * P + P], rqk_l[2 + d][:, j * P:j * P + P])
                        m = mm3(banks[b][:, o:o + T_W[j]], keys, (rqk_h[d][:, j * P:S], rqk_l[d][:, j * P:S]),
                                d == 0, d == 1)
                    m.then_inc(ret_scores, 1)
                proj()
                wait(pe, ret_p_lo, hd * 4 + 4)
                for c in range(4):
                    for j in range(TT):
                        val = (rv_h[j][:, c * P:c * P + P], rv_l[j][:, c * P:c * P + P])
                        sc = (rp_h[:, T_AT[j]:T_AT[j] + T_W[j]], rp_l[:, T_AT[j]:T_AT[j] + T_W[j]])
                        m = mm3(banks[4 + c][:, j * P:S], val, sc, j == 0, j == TT - 1)
                    m.then_inc(ret_pv, 1)
                proj()

                def mean():
                    wait(pe, gn_sum, hd * 6 + 3)
                    pe.matmul(banks[2][:, :], ones[:, :], acc[:, :], start=True, stop=True).then_inc(gn_done, 1)

                proj(hooks={3: mean})
                proj()
                wait(pe, gn_sum, hd * 6 + 6)
                for t in range(TT):
                    m = pe.matmul(banks[3][:, t:t + 1], acc[:, t * P:t * P + P], ones[:, 0:1], start=True, stop=True)
                m.then_inc(gn_done, 1)

            ret_head(Lin(0), True)
            with pe.Fori(0, RH - 1) as i:
                at.enter(i, 16, 20, 16)
                ret_head(Lin(1, 1, i), False)
                at.leave(RH - 1)
            gn_spread(Lin(RH - 1))
            pe.wait_ge(y_lo, 4 * RH)
            ret_out()

            def us(k):
                return uh[k], ul[k]

            def mlp(q, n, base):
                proj(first=[(xl_ready, 8 * q)], hooks={7: lambda: mean_square(n)})
                proj(hooks={4: lambda: spread_rms(n)})
                for _ in range(6):
                    proj()
                with pe.Fori(0, 3) as i:
                    at.enter(i, 16, 16, 16)
                    proj(us, first=[(u_lo, Lin(base, 8, i))])
                    for _ in range(7):
                        proj(us)
                    for _ in range(8):
                        proj()
                    at.leave(3)
                proj(us, first=[(u_lo, base + 24)])
                for _ in range(7):
                    proj(us)

            mlp(1, 1, 0)

            def scores(sm, hd, q, k, half, kind):
                lo, hi = HEAD * half, HEAD * half + HEAD
                if kind == "window":
                    places = [(2, 0), (2, 128), (3, 0), (3, 256)]
                else:
                    places = [(2, 0), (4, 0), (2, 128), (3, 0)]
                for t, (b, o) in enumerate(places):
                    w = (CP_W if kind == "window" else P_W)[t]
                    k0 = (t + 1) * P - w
                    dst = banks[b][:, o:o + w]
                    mm3(dst, (q[0][lo:hi, t * P:t * P + P], q[1][lo:hi, t * P:t * P + P]),
                        (k[0][lo:hi, k0:k0 + w], k[1][lo:hi, k0:k0 + w]), True, False, False)
                    if kind == "window" and w > P:
                        pe.matmul(dst[:, 0:P], sqr[:, 0, :], sqr[:, 3, :], start=False, stop=False,
                                  skip_group_check=True)
                    m = pe.matmul(dst[:, w - P:w], sqr[:, 0, :], sqr[:, 1 if kind == "chunk" else 2, :],
                                  start=False, stop=True, skip_group_check=True)
                m.then_inc(sm.scores, 1)

            def turn(sm, hd, par, kind):
                window = kind == "window"
                wait(pe, sm.probs, hd * 4 + 4)
                wait(pe, sm.o, hd)
                places = [(5, 0), (5, 256), (6, 0), (6, 256)] if window else [(5, 0), (6, 0), (7, 0), (6, 384)]
                for j, (b, o) in enumerate(places):
                    for t in range(j, min(j + 2, TT) if window else TT):
                        k0 = 0 if not window else (t + 1) * P - CP_W[t]
                        src = (CP_AT if window else P_AT)[t] + j * P - k0
                        m = pe.transpose(banks[b][:, o + (t - j) * P:o + (t - j) * P + P],
                                         pf[par][:, src:src + P], ident[:, :])
                m.then_inc(sm.turned, 1)

            def weigh(sm, hd, values, kind):
                window = kind == "window"
                ta, tw = (CT_AT, CT_W) if window else (T_AT, T_W)
                wait(pe, sm.turned_lo, hd * 4 + 4)
                for j in range(TT):
                    m = mm3(banks[7][:, j * P:j * P + tw[j]], values(j),
                            (pt_h[:, ta[j]:ta[j] + tw[j]], pt_l[:, ta[j]:ta[j] + tw[j]]),
                            j == 0, j == TT - 1, False)
                m.then_inc(sm.pv, 1)

            def staged(j):
                return vs_h[:, j * P:j * P + P], vs_l[:, j * P:j * P + P]

            def att_step(s, par, unit=True, late=True, early=True):
                head_par, pair_par = par
                if late:
                    turn(att, s - 1, head_par, "chunk")
                if unit:
                    proj()
                if late:
                    if head_par == 0:
                        wait(pe, stage_lo, (s + 1) // 2)
                    weigh(att, s - 1, staged, "chunk")
                if early:
                    wait(pe, att.qk_lo, s + (3 - head_par))
                    wait(pe, att.biased, (s + 1) * 4)
                    if s.b == -1:
                        pe.wait_ge(masks_ready, 1)
                        pe.wait_ge(squares_landed, 16)
                        pe.wait_ge(att_v, 8)
                    k_of = (ah[pair_par][1], al[pair_par][1])
                    scores(att, s + 1, (ah[pair_par][0], al[pair_par][0]), k_of, head_par, "chunk")

            proj(first=[(xl_ready, 16)], hooks={7: lambda: mean_square(2)})
            proj(hooks={4: lambda: spread_rms(2)})
            for c in range(2):
                if c:
                    wait(pe, att_v, 4)
                for kk in range(4):
                    token_major(kk)
            att_step(Lin(-1), (0, 0), late=False)
            att_step(Lin(0), (1, 0), late=False)
            for j in range(4):
                att_step(Lin(1 + j), (j % 2, (1 + j // 2) % 2))
            with pe.Fori(0, 2) as i:
                at.enter(i, 4, 4, 4)
                for j in range(4):
                    att_step(Lin(5 + j, 4, i), (j % 2, (1 + j // 2) % 2))
                at.leave(2)
            for s in range(13, 17):
                att_step(Lin(s), ((s + 1) % 2, (s + 1) // 2 % 2), unit=False, early=s < 15)
            def attended(k):
                return ao_h[k], ao_l[k]

            proj(attended, first=[(xl_ready, 24)])
            for _ in range(7):
                proj(attended)

            mlp(4, 3, 32)

            mean_square(4)
            spread_rms(4)
            proj(first=[(xl_ready, 40)], hooks={7: lambda: mean_square(5)})
            proj(hooks={4: lambda: spread_rms(5)})
            for kk in range(4):
                token_major(kk)
            slot = at.u % RING
            wait(pe, lo_ready, at.u + 1)
            for t in range(TT):
                wait(pe, hyb_vl, t + 1)
                for k in range(KT):
                    m = mm3(banks[4 + t][:, 0:P], (x_hi[:, k, t * P:t * P + P], x_lo[:, k, t * P:t * P + P]),
                            w_at(slot, k * P, k * P + P), k == 0, k == KT - 1)
            m.then_inc(products_done, 1)
            at.step(1, 0)
            pe.wait_ge(wf_l, 1)
            for k in range(KT):
                m = mm3(banks[2][0:4, :], (wf_hi[:, k, :], wf_lo[:, k, :]), (x_hi[:, k, :], x_lo[:, k, :]),
                        k == 0, k == KT - 1)
            m.then_inc(f_done, 1)

            def hyb_values(p):
                if p < 4:
                    return lambda j: (hv_h[j][:, p * P:p * P + P], hv_l[j][:, p * P:p * P + P])
                return lambda j: (hc_h[:, j * P:j * P + P], hc_l[:, j * P:j * P + P])

            for s in range(-1, 17):
                if 4 <= s < 8:
                    pe.wait_ge(cum_bias, s - 3)
                if s == 1:
                    pe.wait_ge(cum_row, 1)
                if s >= 1:
                    hd = s - 1
                    turn(hyb, Lin(hd), hd % 2, "causal" if hd < 8 else "window")
                if s in HYB_UNITS:
                    proj()
                if s == -1:
                    pe.wait_ge(f_row_ready, 1)
                    for t in range(TT):
                        m = pe.transpose(banks[6][:, 4 * t:4 * t + 4], f_row[:, t * P:t * P + P], ident[0:4, 0:4])
                    m.then_inc(f_done, 1)
                if s >= 1:
                    weigh(hyb, Lin(hd), hyb_values(hd // 2), "causal" if hd < 8 else "window")
                if s < 15:
                    hd = s + 1
                    p = hd // 2
                    wait(pe, hyb.qk_lo, HYB_TILES[p])
                    wait(pe, hyb.biased, 4 * hd)
                    if hd == 0:
                        pe.wait_ge(hyb_vl, 8)
                    kp = p % 2 if p < 4 else 0
                    scores(hyb, hd, (ah[p % 2][0], al[p % 2][0]), (ah[kp][1], al[kp][1]), hd % 2,
                           "causal" if hd < 8 else "window")
                    if 4 <= hd < 8:
                        wait(pe, hyb.turned_lo, 4 * (hd - 2) + 4)
                        pe.matmul(banks[5][:, :], sel_sb[:, (hd - 4) * P:(hd - 3) * P], cum_sb[:, :],
                                  start=True, stop=True).then_inc(cum_bc, 1)
                if s == 0:
                    pe.wait_ge(f_step, 5)
                    pe.wait_ge(tri_landed, 32)
                    for t in range(TT):
                        m = pe.matmul(banks[5][0:4, t * P:S], flog[:, 4 * t:4 * t + 4], tri_sb[:, 0:S - t * P],
                                      start=(t == 0), stop=(t == TT - 1))
                    m.then_inc(cum_done, 1)

            wait(pe, tile_read, at.t)

            def merge_tile(c):
                for g, b in enumerate((0, 1, 5)):
                    wait(pe, gate_read, c * 3 + (g - 2) if c.a else 0)
                    proj(bank=banks[b])
                slot = at.u % RING
                wait(pe, lo_ready, at.u + 1)
                wait(pe, o_lo, 8)
                for g, (a, b) in enumerate(((0, 2), (2, 4), (4, 8))):
                    wait(pe, branch_read, c * 3 + (g - 2) if c.a else 0)
                    for k in range(a, b):
                        m = mm3(banks[2 + g][:, :], w_at(slot, k * P, k * P + P), (oh[k], ol[k]), k == a, k == b - 1)
                m.then_inc(products_done, 1)
                at.step(1, 0)

            merge_tile(Lin(0))
            with pe.Fori(0, KT - 1) as i:
                at.enter(i, 4, 4, 0)
                merge_tile(Lin(1, 1, i))
                at.leave(KT - 1)
            pe.wait_ge(gate_read, 3 * KT)
            def merged_at(k):
                return mg_h[k], mg_l[k]

            proj(merged_at, first=[(xl_ready, 48)])
            for _ in range(7):
                proj(merged_at)

            def down(g):
                first_pair = sum(GROUPS[:g])

                def ss(k):
                    return sh_all[:, (first_pair + k - 1) % 12, :], sl_all[:, (first_pair + k - 1) % 12, :]

                proj(ss, GROUPS[g], first=[(s_lo, first_pair)])
                for _ in range(7):
                    proj(ss, GROUPS[g])

            proj(first=[(xl_ready, 56)], hooks={7: lambda: mean_square(6)})
            proj(hooks={4: lambda: spread_rms(6)})
            proj()
            proj()
            for g in range(3):
                with pe.Fori(0, 3) as i:
                    at.enter(i, 4, 4, 4)
                    for _ in range(4):
                        proj()
                    at.leave(3)
                if g < 2:
                    down(g)
            for _ in range(4):
                proj()
            down(2)
            down(3)
            assert at.u.b == N_UNITS
            mean_square(7)
            spread_rms(7)

        @block.scalar
        def _(act):
            hold = holder(xh_ready)
            at = Place()

            def split(ahead=LEAD):
                u = at.u + ahead
                if u.a == 0 and u.b >= N_UNITS:
                    return
                wait(act, raw_landed[u % RING], (u // RING + 1) * 16)
                wait(act, products_done, at.pe)
                act.activation(w_hi[:, u % RING, :], raw[:, u % RING, :], ACT.Copy).then_inc(hi_ready, 1)

            def hi_and_square(q, n, j, gain, ready, count):
                wait(act, ready, count)
                act.activation(x_hi[:, j, :], h[:, j, :], ACT.Copy, scale=col(gain + j)).then_inc(xh_ready, 1)
                if j >= 4:
                    wait(act, acc_sum, 6 * n + max(1, j - 4))
                act.activation(sq[:, j % 4, :], h[:, j, :], ACT.Square).then_inc(sq_ready, 1)

            def square_only(n, j, ready, count):
                wait(act, ready, count)
                if j >= 4:
                    wait(act, acc_sum, 6 * n + max(1, j - 4))
                act.activation(sq[:, j % 4, :], h[:, j, :], ACT.Square).then_inc(sq_ready, 1)

            def root(n):
                wait(act, ms_ready, n + 1)
                act.activation(sd, ms, ACT.Sqrt).then_inc(sd_ready, 1)

            def keep_rms(n):
                wait(act, stat_done, 2 * n + 2)
                act.activation(rbc[:, :], banks[3][:, :], ACT.Copy).then_inc(rbc_ready, 1)

            for j in range(KT):
                act.dma_start(h[:, j, :], x_t[j * P:(j + 1) * P, :]).then_inc(x_landed[j], 16)
                if j == 0:
                    act.dma_start(colv[:, :], cols).then_inc(cols_landed, 16)
            act.dma_start(cosr, c_rope[0]).then_inc(rope_landed, 16)
            act.dma_start(sinr, c_rope[1]).then_inc(rope_landed, 16)
            act.wait_ge(cols_landed, 16)
            hi_and_square(0, 0, 0, C_MIX0, x_landed[0], 16)
            for n in range(LEAD):
                split(n)
                hi_and_square(0, 0, n + 1, C_MIX0, x_landed[n + 1], 16)
            for j in range(4, KT):
                hi_and_square(0, 0, j, C_MIX0, x_landed[j], 16)
            act.wait_ge(masks_landed, 16)
            act.activation(sqr[:, :, :], masks_sb, ACT.Copy).then_inc(masks_ready, 1)

            def rope_his(hd, x):
                for c in range(2):
                    wait(act, rope_ready, hd * 4 + (2 * x + c + 1))
                    act.activation(rqk_h[2 * x + c], qkf[c], ACT.Copy).then_inc(rope_hi, 1)

            def y_his(hd):
                for c in range(4):
                    wait(act, y_ready, hd * 4 + (c + 1))
                    act.activation(ry_h[c], oc[c], ACT.Copy).then_inc(y_hi, 1)

            def gate(hd, c):
                wait(act, tile_read, at.t)
                act.activation(sg[c], sg[c], ACT.Silu).then_inc(gate_ready, 1)

            def ret_head(hd, first):
                split()
                if first:
                    root(0)
                    keep_rms(0)
                    act.wait_ge(strip_saved, 16)
                at.step()
                split()
                if not first:
                    y_his(hd - 1)
                at.step()
                rope_his(hd, 0)
                split()
                at.step()
                split()
                at.step()
                rope_his(hd, 1)
                for kk in range(4):
                    split()
                    at.step(1, 0)
                wait(act, products_done, at.pe)
                for t in range(TT):
                    act.activation(rv_h[t], banks[4 + t][:, :], ACT.Copy, scale=rcol[:, t:t + 1]).then_inc(v_hi, 1)
                if not first:
                    for _ in range(4):
                        split()
                        at.step(2, 2)
                split()
                for j in range(4):
                    wait(act, ret_p, hd * 4 + (j + 1))
                    act.activation(rp_h[:, T_AT[j]:T_AT[j] + T_W[j]], pf_ret[:, T_AT[j]:T_AT[j] + T_W[j]],
                                   ACT.Copy).then_inc(ret_p_hi, 1)
                at.step()
                gate(hd, 0)
                split()
                for c in range(4):
                    wait(act, ret_pv, hd * 4 + (c + 1))
                    act.activation(oc[c], banks[4 + c][:, :], ACT.Copy).then_inc(ret_o, 1)
                at.step()
                gate(hd, 1)
                split()
                for c in range(4):
                    wait(act, gn_centred, hd * 4 + (c + 1))
                    act.activation(sq[:, c, :], oc[c], ACT.Square).then_inc(gn_sq, 1)
                at.step()
                gate(hd, 2)
                split()
                at.step()
                gate(hd, 3)
                wait(act, gn_ms_r, hd + 1)
                act.activation(gn_sd, gn_ms, ACT.Sqrt).then_inc(gn_sd_r, 1)

            ret_head(Lin(0), True)
            with act.Fori(0, RH - 1) as i:
                at.enter(i, 16, 20, 16)
                ret_head(Lin(1, 1, i), False)
                at.leave(RH - 1)
            y_his(Lin(RH - 1))

            def last_tiles(q, n, gain, per_unit, final=False):
                for j in range(KT):
                    if j % per_unit == 0:
                        split()
                        at.u = at.u + 1
                    at.pe, at.t = at.pe + 1, at.t + 1
                    if final:
                        square_only(n, j, tile_read, at.t)
                    else:
                        hi_and_square(q, n, j, gain, tile_read, at.t)

            last_tiles(1, 1, C_MLP0, 2)

            def mlp_up(base):
                for j in range(KT):
                    split()
                    at.step()
                    wait(act, u_ready, lin(base) + (j + 1))
                    act.activation(uh[j], uf[j % 2], ACT.Copy).then_inc(u_hi, 1)

            def mlp(n, base):
                root(n)
                keep_rms(n)
                mlp_up(base)
                with act.Fori(0, 3) as i:
                    at.enter(i, 16, 16, 16)
                    for j in range(KT):
                        split()
                        at.step()
                    mlp_up(Lin(base + 8, 8, i))
                    at.leave(3)

            mlp(1, 0)
            last_tiles(2, 2, C_MIX1, 1)

            def exps(sm, hd, par, window=False):
                hold(act, (sm.negmax, hd + 1))
                for t in range(TT):
                    a, w = (CP_AT[t], CP_W[t]) if window else (P_AT[t], P_W[t])
                    act.activation(pf[par][:, a:a + w], pf[par][:, a:a + w], ACT.Exp, bias=nm[par][:, t:t + 1],
                                   accum_out=sums[par][:, t:t + 1]).then_inc(sm.exp, 1)

            def turned_his(sm, hd, window=False):
                wait(act, sm.turned, hd + 1)
                places = [(5, 0), (5, 256), (6, 0), (6, 256)] if window else [(5, 0), (6, 0), (7, 0), (6, 384)]
                for j, (b, o) in enumerate(places):
                    a, w = (CT_AT[j], CT_W[j]) if window else (T_AT[j], T_W[j])
                    act.activation(pt_h[:, a:a + w], banks[b][:, o:o + w], ACT.Copy).then_inc(sm.turned_hi, 1)

            def qk_hi(sm, dst):
                wait(act, tile_read, at.t)
                act.activation(dst, af[0], ACT.Copy).then_inc(sm.qk_hi, 1)

            def att_step(s, head_par, pair_par, unit_dst=None, late=True, early=True, pair=None):
                if late:
                    if head_par == 0:
                        hold(act, (att.pv, s - 1))
                        act.activation(vs_h, pair_tile(pair), ACT.Copy).then_inc(stage_hi, 1)
                    turned_his(att, s - 1)
                if unit_dst is not None:
                    split()
                    at.step()
                if early:
                    exps(att, s, 1 - head_par)
                if unit_dst is not None:
                    qk_hi(att, unit_dst)
                if late:
                    lo = HEAD * head_par
                    hold(act, (att.pv, s))
                    act.activation(pair_tile(pair, lo, lo + HEAD), banks[7][lo:lo + HEAD, :], ACT.Copy).then_inc(att.o, 1)

            root(2)
            keep_rms(2)
            split()
            at.step()
            qk_hi(att, ah[0][0])
            split()
            at.step()
            qk_hi(att, ah[0][1])
            for c in range(2):
                for kk in range(4):
                    split()
                    at.step(1, 0)
                wait(act, products_done, at.pe)
                for t in range(TT):
                    act.activation(vf[:, 4 * c:4 * c + 4, t, :],
                                   banks[4 + t][:, :].rearrange("p (a d) -> p a d", a=4), ACT.Copy,
                                   scale=rcol[:, t:t + 1]).then_inc(att_v, 1)
            att_step(Lin(-1), 0, 0, ah[1][0], late=False, early=False)
            att_step(Lin(0), 1, 0, ah[1][1], late=False)
            for j in range(4):
                att_step(Lin(1 + j), j % 2, None, ah[(j // 2) % 2][j % 2], pair=Lin(j // 2))
            with act.Fori(0, 2) as i:
                at.enter(i, 4, 4, 4)
                for j in range(4):
                    att_step(Lin(5 + j, 4, i), j % 2, None, ah[(j // 2) % 2][j % 2], pair=Lin(2 + j // 2, 2, i))
                at.leave(2)
            for s in range(13, 17):
                att_step(Lin(s), (s + 1) % 2, None, late=True, early=s < 16, pair=Lin((s - 1) // 2))
            for j in range(KT):
                wait(act, att.o, 2 * j + 2)
                act.activation(ao_h[j], of[j], ACT.Copy).then_inc(xh_ready, 1)
            last_tiles(4, 3, C_MLP1, 1)
            mlp(3, 32)
            last_tiles(None, 4, None, 1, final=True)

            root(4)
            keep_rms(4)
            for j in range(KT):
                hi_and_square(5, 5, j, C_LN1, hn_ready, j + 1)
            root(5)
            keep_rms(5)
            split()
            at.step()
            qk_hi(hyb, ah[0][0])
            split()
            at.step()
            qk_hi(hyb, ah[0][1])
            for kk in range(4):
                split()
                at.step(1, 0)
            wait(act, products_done, at.pe)
            for t in range(TT):
                act.activation(hv_h[t], banks[4 + t][:, :], ACT.Copy, scale=rcol[:, t:t + 1]).then_inc(hyb_vh, 1)
            act.activation(wf_hi[:, :, :], wf_raw[:, :, :], ACT.Copy).then_inc(wf_h, 1)
            split()
            at.step(1, 0)
            wait(act, products_done, at.pe)
            for t in range(TT):
                act.activation(hc_h[:, t * P:t * P + P], banks[4 + t][:, 0:P], ACT.Copy,
                               scale=rcol[:, t:t + 1]).then_inc(hyb_vh, 1)
            for s in range(-1, 17):
                if s >= 1:
                    turned_his(hyb, Lin(s - 1), s - 1 >= 8)
                if s in HYB_UNITS:
                    split()
                    at.step()
                if 0 <= s < 16:
                    if s >= 8:
                        par = s % 2
                        act.wait_ge(hyb.negmax, s + 1)
                        act.activation(es[par], nm[par], ACT.Exp, bias=sink_b[:, SINK_OF[s - 8]:SINK_OF[s - 8] + 1])\
                            .then_inc(sink_exp, 1)
                    exps(hyb, Lin(s), s % 2, s >= 8)
                if s in HYB_UNITS:
                    n, dst = HYB_UNITS[s]
                    qk_hi(hyb, ah[dst[0]][dst[1]])
                if s == -1:
                    act.wait_ge(f_step, 2)
                    act.activation(fe, fn, ACT.Exp).then_inc(f_act, 1)
                if s == 0:
                    act.wait_ge(f_step, 3)
                    act.activation(fn, fe, ACT.Ln).then_inc(f_act, 1)
                    act.wait_ge(cum_done, 1)
                    act.activation(cum_sb, banks[5][0:4, :], ACT.Copy, scale=-1.0).then_inc(cum_row, 1)
                if s >= 1:
                    hd = s - 1
                    lo = HEAD * (hd % 2)
                    act.wait_ge(hyb.pv, s)
                    act.activation(of[hd // 2][lo:lo + HEAD, :], banks[7][lo:lo + HEAD, :], ACT.Copy)\
                        .then_inc(hyb.o, 1)
                if 4 <= s + 1 < 8:
                    act.wait_ge(cum_bc, s + 1 - 3)
                    act.activation(bias[(s + 1) % 2], banks[5][:, :], ACT.Copy).then_inc(cum_bias, 1)
            act.wait_ge(hyb.o, 16)
            for j in range(KT):
                act.activation(oh[j], of[j], ACT.Copy).then_inc(o_hi, 1)

            def merged_hi(c):
                wait(act, merged, c + 1)
                act.activation(mg_h[c.b] if not c.a else arena_r[:, bass.ds((c * S + 16 * S).val(), S)],
                               mf_at(c), ACT.Copy).then_inc(xh_ready, 1)

            def merge_tile(c):
                for g in range(3):
                    split()
                    at.step(1, 0)
                    wait(act, gate_read, c * 3 + (g + 1))
                    act.activation(gf[g], gf[g], ACT.Sigmoid).then_inc(gate_sig, 1)
                    if g == 0 and (c.a or c.b):
                        merged_hi(c - 1)
                split()
                at.step(1, 0)

            merge_tile(Lin(0))
            with act.Fori(0, KT - 1) as i:
                at.enter(i, 4, 4, 0)
                merge_tile(Lin(1, 1, i))
                at.leave(KT - 1)
            merged_hi(Lin(KT - 1))
            last_tiles(7, 6, C_LN2, 1)
            root(6)
            keep_rms(6)

            def his(pair):
                tile = (pair - 1).fold(12)
                hold(act, (s_ready, pair + 1))
                act.activation(sh_all[:, bass.ds(tile.val(), 1), :].rearrange("p a n -> p (a n)"), sf[pair.b % 2],
                               ACT.Copy).then_inc(s_hi, 1)

            def glu_pair(pair, first=False):
                for n in range(2):
                    split()
                    at.step()
                    hold(act, (tile_read, at.t))
                    k = pair + n * PAIRS
                    act.activation(cy[2 * (pair.b % 2) + n], cz[2 * (pair.b % 2) + n][:, 2:S + 2], ACT.Identity,
                                   scale=col(k + (C_CW + 2 * 2 * PAIRS)), bias=col(k + C_CB)).then_inc(conv_0, 1)
                if not first:
                    his(pair - 1)
                y = cy[2 * (pair.b % 2)]
                wait(act, conv_2, pair * 2 + 1)
                act.activation(y, y, ACT.Silu).then_inc(silu_done, 1)

            glu_pair(Lin(0), True)
            glu_pair(Lin(1))
            for g in range(3):
                with act.Fori(0, 3) as i:
                    at.enter(i, 4, 4, 4)
                    for j in range(2):
                        glu_pair(Lin(2 + 6 * g + j, 2, i))
                    at.leave(3)
                if g < 2:
                    for j in range(KT):
                        split()
                        at.step()
            glu_pair(Lin(PAIRS - 2))
            glu_pair(Lin(PAIRS - 1))
            his(Lin(PAIRS - 1))
            for j in range(KT):
                split()
                at.step()
            last_tiles(None, 7, None, 1, final=True)
            root(7)
            keep_rms(7)

        @block.vector
        def _(dve):
            hold = holder(xh_ready)
            at = Place()

            def split(ahead=LEAD):
                u = at.u + ahead
                if u.a == 0 and u.b >= N_UNITS:
                    return
                wait(dve, hi_ready, u + 1)
                s = u % RING
                dve.tensor_tensor(w_lo[:, s, :], raw[:, s, :], f32(w_hi[:, s, :]), ALU.subtract).then_inc(lo_ready, 1)

            def x_lo_of(q, j, gain):
                wait(dve, xh_ready, 8 * q + j + 1)
                dve.scalar_tensor_tensor(x_lo[:, j, :], h[:, j, :], col(gain + j), f32(x_hi[:, j, :]),
                                         ALU.mult, ALU.subtract).then_inc(xl_ready, 1)

            def rms(n):
                wait(dve, stat_done, 2 * n + 1)
                dve.tensor_scalar(ms, banks[2][:, 0:4], 1.0 / D, EPS, ALU.mult, ALU.add).then_inc(ms_ready, 1)
                wait(dve, sd_ready, n + 1)
                dve.reciprocal(rcol, sd).then_inc(rcol_ready, 1)
                wait(dve, rcol_ready, n + 1)
                make_diag(rcol).then_inc(diag_ready, 1)

            def make_diag(r):
                return dve.tensor_tensor(diag[:, :, :], ident[:, :].unsqueeze(1).broadcast_to([P, TT, P]),
                                         r.unsqueeze(2).broadcast_to([P, TT, P]), ALU.mult)

            def scaled(dst, n_bank=None):
                wait(dve, products_done, at.pe)
                return dve.tensor_tensor(dst, banks[(at.t - 1) % 2][:, :], rbc[:, :], ALU.mult)

            def add_tile(j):
                wait(dve, products_done, at.pe)
                dve.tensor_tensor(h[:, j, :], banks[(at.t - 1) % 2][:, :], h[:, j, :], ALU.add).then_inc(tile_read, 1)

            dve.memset(ones[:, :], 1.0).then_inc(consts_made, 1)
            dve.wait_ge(cols_landed, 16)
            for j in range(KT):
                dve.wait_ge(x_landed[j], 16)
                x_lo_of(0, j, C_MIX0)
                if j < LEAD:
                    split(j)
            dve.wait_ge(strip_made, 1)
            dve.tensor_copy(strip_sb[:, 0:512], banks[6][0:12, 0:512])
            dve.tensor_copy(strip_sb[:, 512:640], banks[7][0:12, 0:128]).then_inc(strip_copied, 1)

            def y_of(hd):
                wait(dve, gn_done, hd * 3 + 3)
                for c in range(4):
                    dve.scalar_tensor_tensor(oc[c], oc[c], col(hd * 4 + (C_GN + c)), banks[2][:, :],
                                             ALU.mult, ALU.mult).then_inc(y_scaled, 1)
                for c in range(4):
                    wait(dve, gate_ready, hd * 4 + 4)
                    wait(dve, y_scaled, hd * 4 + (c + 1))
                    dve.tensor_tensor(oc[c], oc[c], sg[c], ALU.mult).then_inc(y_ready, 1)

            def rotate(hd, x, part, between=None):
                wait(dve, products_done, at.pe)
                src = banks[(at.t - 1) % 2][:, :]
                if part == 0:
                    dve.tensor_tensor(rt[0], src, cosr, ALU.mult)
                    dve.tensor_tensor(rt[1], src, sinr, ALU.mult).then_inc(tile_read, 1)
                    return
                dve.tensor_tensor(rt[2], src, sinr, ALU.mult)
                dve.tensor_tensor(rt[3], src, cosr, ALU.mult).then_inc(tile_read, 1)
                wait(dve, rope_lo, hd * 4 + 2 * x)
                wait(dve, tile_read, at.t)
                dve.tensor_tensor(qkf[0], rt[0], rt[2], ALU.subtract).then_inc(rope_ready, 1)
                dve.tensor_tensor(qkf[1], rt[1], rt[3], ALU.add).then_inc(rope_ready, 1)

            def ret_head(hd, first):
                split()
                if first:
                    dve.wait_ge(squares_landed, 16)
                    rms(0)
                    dve.wait_ge(rbc_ready, 1)
                    dve.wait_ge(rope_landed, 32)
                    dve.tensor_tensor(cosr, cosr, rbc[:, :], ALU.mult)
                    dve.tensor_tensor(sinr, sinr, rbc[:, :], ALU.mult).then_inc(rope_tables, 1)
                    dve.wait_ge(rope_tables, 1)
                    dve.wait_ge(masks_ready, 1)
                at.step()
                wait(dve, ret_p_lo, hd * 4)
                rotate(hd, 0, 0)
                split()
                if not first:
                    y_of(hd - 1)
                at.step()
                rotate(hd, 0, 1)
                split()
                at.step()
                rotate(hd, 1, 0)
                split()
                at.step()
                rotate(hd, 1, 1)
                for kk in range(4):
                    split()
                    at.step(1, 0)
                for t in range(TT):
                    wait(dve, v_hi, hd * 4 + (t + 1))
                    dve.scalar_tensor_tensor(rv_l[t], banks[4 + t][:, :], rcol[:, t:t + 1], f32(rv_h[t]),
                                             ALU.mult, ALU.subtract).then_inc(v_lo, 1)
                if not first:
                    for n in range(4):
                        split()
                        for c in range(2):
                            at.pe, at.t = at.pe + 1, at.t + 1
                            add_tile(2 * n + c)
                        at.u = at.u + 1
                wait(dve, decay_landed, (hd + 1) * 16)
                for j, (b, o) in enumerate([(2, 0), (3, 0), (4, 0), (4, 256)]):
                    wait(dve, ret_scores, hd * 4 + (j + 1 if j != 2 else 4))
                    dve.tensor_tensor(pf_ret[:, T_AT[j]:T_AT[j] + T_W[j]], banks[b][:, o:o + T_W[j]],
                                      decay[:, 0:T_W[j]], ALU.mult).then_inc(ret_p, 1)
                for c in range(4):
                    split()
                    if c == 2:
                        wait(dve, gn_done, hd * 3 + 1)
                        for e in range(4):
                            dve.scalar_tensor_tensor(oc[e], banks[2][:, :], -1.0 / RV, oc[e],
                                                     ALU.mult, ALU.add).then_inc(gn_centred, 1)
                    at.step()
                    scaled(sg[c]).then_inc(tile_read, 1)
                wait(dve, gn_done, hd * 3 + 2)
                dve.tensor_scalar(gn_ms, banks[3][:, 0:4], 1.0 / RV, EPS, ALU.mult, ALU.add).then_inc(gn_ms_r, 1)
                wait(dve, gn_sd_r, hd + 1)
                dve.reciprocal(gn_r, gn_sd).then_inc(gn_r_r, 1)
                wait(dve, gn_r_r, hd + 1)
                make_diag(gn_r).then_inc(gn_diag, 1)

            ret_head(Lin(0), True)
            with dve.Fori(0, RH - 1) as i:
                at.enter(i, 16, 20, 16)
                ret_head(Lin(1, 1, i), False)
                at.leave(RH - 1)
            y_of(Lin(RH - 1))

            def last_tiles(q, gain, per_unit):
                for j in range(KT):
                    if j % per_unit == 0:
                        split()
                        at.u = at.u + 1
                    at.pe, at.t = at.pe + 1, at.t + 1
                    add_tile(j)
                    if q is not None:
                        x_lo_of(q, j, gain)

            last_tiles(1, C_MLP0, 2)

            def mlp_up(base):
                for j in range(KT):
                    split()
                    at.step()
                    scaled(zf[j % 2]).then_inc(tile_read, 1)
                    wait(dve, tile_read, at.t)
                    dve.scalar_tensor_tensor(uf[j % 2], zf[j % 2], 0.0, zf[j % 2], ALU.max, ALU.mult)\
                        .then_inc(u_ready, 1)
                    wait(dve, u_hi, lin(base) + (j + 1))
                    dve.tensor_tensor(ul[j], uf[j % 2], f32(uh[j]), ALU.subtract).then_inc(u_lo, 1)

            def mlp(n, base):
                rms(n)
                dve.wait_ge(rbc_ready, n + 1)
                mlp_up(base)
                with dve.Fori(0, 3) as i:
                    at.enter(i, 16, 16, 16)
                    for j in range(KT):
                        split()
                        at.step()
                        add_tile(j)
                    mlp_up(Lin(base + 8, 8, i))
                    at.leave(3)

            mlp(1, 0)
            last_tiles(2, C_MIX1, 1)

            def maxima(sm, hd, par, n_bias, kind, sink=None):
                hold(dve, (sm.scores, hd + 1), *([(sm.bias[par], n_bias)] if n_bias is not None else []))
                window = kind == "window"
                places = [(2, 0), (2, 128), (3, 0), (3, 256)] if window else [(2, 0), (4, 0), (2, 128), (3, 0)]
                for t, (b, o) in enumerate(places):
                    a, w = (CP_AT[t], CP_W[t]) if window else (P_AT[t], P_W[t])
                    if window:
                        bt = bias[par][:, 256 - w:256]
                    elif kind == "key":
                        bt = bias[par][:, 0:w]
                    else:
                        bt = bias[par][:, S - w:S]
                    dve.tensor_tensor_reduce(pf[par][:, a:a + w], banks[b][:, o:o + w], bt, 1.0, LOWEST,
                                             ALU.add, ALU.max, mx[par][:, t:t + 1]).then_inc(sm.biased, 1)
                wait(dve, sm.biased, hd * 4 + 4)
                if sink is None:
                    dve.tensor_scalar(nm[par], mx[par], -1.0, None, ALU.mult).then_inc(sm.negmax, 1)
                else:
                    dve.tensor_scalar(nm[par], mx[par], -1.0, nsink[:, sink:sink + 1], ALU.mult, ALU.min)\
                        .then_inc(sm.negmax, 1)

            def turned_los(sm, hd, window=False):
                places = [(5, 0), (5, 256), (6, 0), (6, 256)] if window else [(5, 0), (6, 0), (7, 0), (6, 384)]
                for j, (b, o) in enumerate(places):
                    a, w = (CT_AT[j], CT_W[j]) if window else (T_AT[j], T_W[j])
                    wait(dve, sm.turned_hi, hd * 4 + ((2, 2, 4, 4) if window else (1, 4, 4, 4))[j])
                    dve.tensor_tensor(pt_l[:, a:a + w], banks[b][:, o:o + w], f32(pt_h[:, a:a + w]),
                                      ALU.subtract).then_inc(sm.turned_lo, 1)

            def inverse(sm, hd, par):
                wait(dve, sm.exp, hd * 4 + 4)
                dve.reciprocal(rinv[par], sums[par]).then_inc(sm.rinv, 1)

            def qk_tile(sm, n, scale, dst):
                wait(dve, sm.qk_lo, n)
                wait(dve, products_done, at.pe)
                dve.scalar_tensor_tensor(af[0], banks[(at.t - 1) % 2][:, :], scale, rbc[:, :], ALU.mult, ALU.mult)\
                    .then_inc(tile_read, 1)
                wait(dve, sm.qk_hi, lin(n) + 1)
                dve.tensor_tensor(dst[1], af[0], f32(dst[0]), ALU.subtract).then_inc(sm.qk_lo, 1)

            def att_step(s, head_par, unit=None, late=True, early=True, pair=None):
                if early:
                    hd = s
                    count = Lin((hd.b // 2 + 1) * 16, hd.a * 8, hd.i)
                    maxima(att, hd, 1 - head_par, count, "rel")
                if late:
                    if head_par == 0:
                        wait(dve, stage_hi, (s + 1) // 2)
                        dve.tensor_tensor(vs_l, pair_tile(pair), f32(vs_h), ALU.subtract).then_inc(stage_lo, 1)
                    turned_los(att, s - 1)
                if unit is not None:
                    split()
                if early:
                    inverse(att, s, 1 - head_par)
                if unit is not None:
                    at.step()
                    qk_tile(att, s + 3, SCALE if unit[1] == 0 else 1.0, (ah[unit[0]][unit[1]], al[unit[0]][unit[1]]))

            rms(2)
            dve.wait_ge(rbc_ready, 3)
            for n in range(2):
                split()
                at.step()
                qk_tile(att, n, (SCALE, 1.0)[n], (ah[0][n], al[0][n]))
            for _ in range(8):
                split()
                at.step(1, 0)
            att_step(Lin(-1), 0, (1, 0), late=False, early=False)
            att_step(Lin(0), 1, (1, 1), late=False)
            for j in range(4):
                att_step(Lin(1 + j), j % 2, ((j // 2) % 2, j % 2), pair=Lin(j // 2))
            with dve.Fori(0, 2) as i:
                at.enter(i, 4, 4, 4)
                for j in range(4):
                    att_step(Lin(5 + j, 4, i), j % 2, ((j // 2) % 2, j % 2), pair=Lin(2 + j // 2, 2, i))
                at.leave(2)
            for s in range(13, 17):
                att_step(Lin(s), (s + 1) % 2, None, early=s < 16, pair=Lin((s - 1) // 2))
            for j in range(KT):
                wait(dve, xh_ready, 24 + j + 1)
                dve.tensor_tensor(ao_l[j], of[j], f32(ao_h[j]), ALU.subtract).then_inc(xl_ready, 1)
            last_tiles(4, C_MLP1, 1)
            mlp(3, 32)
            last_tiles(None, None, 1)

            rms(4)
            dve.wait_ge(rbc_ready, 5)
            for j in range(KT):
                dve.scalar_tensor_tensor(h[:, j, :], h[:, j, :], col(C_FIN + j), rbc[:, :], ALU.mult, ALU.mult)\
                    .then_inc(hn_ready, 1)
                if j:
                    x_lo_of(5, j - 1, C_LN1)
            x_lo_of(5, KT - 1, C_LN1)
            rms(5)
            dve.wait_ge(rbc_ready, 6)
            for n in range(2):
                split()
                at.step()
                qk_tile(hyb, n, (SCALE, 1.0)[n], (ah[0][n], al[0][n]))
            for _ in range(4):
                split()
                at.step(1, 0)
            for t in range(TT):
                wait(dve, hyb_vh, t + 1)
                dve.scalar_tensor_tensor(hv_l[t], banks[4 + t][:, :], rcol[:, t:t + 1], f32(hv_h[t]),
                                         ALU.mult, ALU.subtract).then_inc(hyb_vl, 1)
            dve.wait_ge(wf_h, 1)
            dve.tensor_tensor(wf_lo[:, :, :], wf_raw[:, :, :], f32(wf_hi[:, :, :]), ALU.subtract).then_inc(wf_l, 1)
            dve.wait_ge(small_in, 48)
            dve.tensor_scalar(nsink, sink_b, -1.0, None, ALU.mult).then_inc(sink_ready, 1)
            split()
            at.step(1, 0)
            for t in range(TT):
                wait(dve, hyb_vh, 4 + t + 1)
                dve.scalar_tensor_tensor(hc_l[:, t * P:t * P + P], banks[4 + t][:, 0:P], rcol[:, t:t + 1],
                                         f32(hc_h[:, t * P:t * P + P]), ALU.mult, ALU.subtract).then_inc(hyb_vl, 1)
            dve.wait_ge(f_done, 1)
            dve.tensor_tensor(f_row, banks[2][0:4, :], rbc[0:4, :], ALU.mult).then_inc(f_row_ready, 1)
            for s in range(-1, 17):
                if 0 <= s < 16:
                    kind = "rel" if s < 4 else "key" if s < 8 else "window"
                    if 4 <= s < 8:
                        dve.wait_ge(cum_bias, s - 3)
                    if s == 8:
                        dve.wait_ge(sink_ready, 1)
                    maxima(hyb, Lin(s), s % 2, BIAS_COUNT[s], kind, None if s < 8 else SINK_OF[s - 8])
                if s == 0:
                    dve.wait_ge(f_act, 1)
                    dve.tensor_scalar(fe, fe, 1.0, None, ALU.add).then_inc(f_step, 1)
                    dve.wait_ge(f_step, 2)
                    dve.tensor_scalar(fl, fl, 0.0, None, ALU.min).then_inc(f_step, 1)
                if s >= 1:
                    turned_los(hyb, Lin(s - 1), s - 1 >= 8)
                if s in HYB_UNITS:
                    split()
                if 0 <= s < 8:
                    inverse(hyb, Lin(s), s % 2)
                elif 8 <= s < 16:
                    dve.wait_ge(hyb.exp, 4 * s + 4)
                    dve.wait_ge(sink_exp, s - 7)
                    dve.tensor_tensor(sums2[s % 2], sums[s % 2], es[s % 2], ALU.add).then_inc(sink_sum, 1)
                    dve.wait_ge(sink_sum, s - 7)
                    dve.reciprocal(rinv[s % 2], sums2[s % 2]).then_inc(hyb.rinv, 1)
                if s in HYB_UNITS:
                    n, (a, b) = HYB_UNITS[s]
                    at.step()
                    qk_tile(hyb, n, SCALE if b == 0 else 1.0, (ah[a][b], al[a][b]))
                if s == -1:
                    dve.wait_ge(f_done, 2)
                    dve.tensor_tensor(fl.rearrange("p (t a) -> p t a", t=TT),
                                      banks[6][:, 0:16].rearrange("p (t a) -> p t a", t=TT),
                                      fb_b.unsqueeze(1).broadcast_to([P, TT, 4]), ALU.add).then_inc(f_step, 1)
                    dve.wait_ge(f_step, 1)
                    dve.scalar_tensor_tensor(fn, fl, -1.0, fl, ALU.mult, ALU.min).then_inc(f_step, 1)
                if s == 0:
                    dve.wait_ge(f_act, 2)
                    dve.wait_ge(f_step, 4)
                    dve.tensor_tensor(flog, fl, fn, ALU.subtract).then_inc(f_step, 1)
            for j in range(KT):
                wait(dve, o_hi, j + 1)
                dve.tensor_tensor(ol[j], of[j], f32(oh[j]), ALU.subtract).then_inc(o_lo, 1)

            def merged_lo(c):
                wait(dve, xh_ready, c + (48 + 1))
                if c.a:
                    hi, lo = (arena_r[:, bass.ds((c * S + n * S).val(), S)] for n in (16, 24))
                else:
                    hi, lo = mg_h[c.b], mg_l[c.b]
                dve.tensor_tensor(lo, mf_at(c), f32(hi), ALU.subtract).then_inc(xl_ready, 1)

            def merge_tile(c, with_lo=True):
                for g, b in enumerate((0, 1, 5)):
                    split()
                    at.step(1, 0)
                    wait(dve, products_done, at.pe)
                    dve.tensor_tensor(gf[g], banks[b][:, :], rbc[:, :], ALU.mult).then_inc(gate_read, 1)
                    if g == 1 and with_lo:
                        merged_lo(c - 1)
                split()
                at.step(1, 0)
                wait(dve, products_done, at.pe)
                for g in range(3):
                    wait(dve, gate_sig, c * 3 + (g + 1))
                    dve.tensor_tensor(mt[g], banks[2 + g][:, :], gf[g], ALU.mult).then_inc(branch_read, 1)
                wait(dve, branch_read, c * 3 + 3)
                dve.tensor_tensor(mt[3], mt[0], mt[1], ALU.add).then_inc(merge_a, 1)
                wait(dve, merge_a, c + 1)
                dve.tensor_tensor(mf_at(c), mt[3], mt[2], ALU.add).then_inc(merged, 1)

            merge_tile(Lin(0), False)
            with dve.Fori(0, 5) as i:
                at.enter(i, 4, 4, 0)
                merge_tile(Lin(1, 1, i))
                at.leave(5)
            merge_tile(Lin(6), False)
            merge_tile(Lin(7), False)
            for c in range(5, 8):
                merged_lo(Lin(c))
            last_tiles(7, C_LN2, 1)
            rms(6)
            dve.wait_ge(rbc_ready, 7)

            for n in range(4):
                m = dve.memset(cz[n][:, 0:2], 0.0)
            m.then_inc(pad_made, 1)
            dve.wait_ge(pad_made, 1)

            def taps(pair, n):
                par = pair.b % 2
                z, y, k = cz[2 * par + n], cy[2 * par + n], pair + n * PAIRS
                wait(dve, conv_0, pair * 2 + (n + 1))
                dve.scalar_tensor_tensor(y, z[:, 1:S + 1], col(k + (C_CW + 2 * PAIRS)), y, ALU.mult, ALU.add)\
                    .then_inc(conv_1, 1)
                wait(dve, conv_1, pair * 2 + (n + 1))
                dve.scalar_tensor_tensor(y, z[:, 0:S], col(k + C_CW), y, ALU.mult, ALU.add).then_inc(conv_2, 1)

            def product(pair):
                par = pair.b % 2
                wait(dve, silu_done, pair + 1)
                wait(dve, conv_2, pair * 2 + 2)
                dve.tensor_tensor(sf[par], cy[2 * par], cy[2 * par + 1], ALU.mult).then_inc(s_ready, 1)

            def los(pair):
                at_12 = bass.ds((pair - 1).fold(12).val(), 1)
                wait(dve, s_hi, pair + 1)
                dve.tensor_tensor(sl_all[:, at_12, :].rearrange("p a n -> p (a n)"), sf[pair.b % 2],
                                  f32(sh_all[:, at_12, :].rearrange("p a n -> p (a n)")), ALU.subtract)\
                    .then_inc(s_lo, 1)

            def glu_pair(pair, first=False):
                for n in range(2):
                    split()
                    at.step()
                    scaled(cz[2 * (pair.b % 2) + n][:, 2:S + 2]).then_inc(tile_read, 1)
                    if n == 0 and not first:
                        taps(pair - 1, 1)
                    if n == 1:
                        if not first:
                            product(pair - 1)
                        taps(pair, 0)
                        if not first:
                            los(pair - 1)

            glu_pair(Lin(0), True)
            glu_pair(Lin(1))
            for g in range(3):
                with dve.Fori(0, 3) as i:
                    at.enter(i, 4, 4, 4)
                    for j in range(2):
                        glu_pair(Lin(2 + 6 * g + j, 2, i))
                    at.leave(3)
                if g < 2:
                    for j in range(KT):
                        split()
                        at.step()
                        add_tile(j)
            glu_pair(Lin(PAIRS - 2))
            glu_pair(Lin(PAIRS - 1))
            taps(Lin(PAIRS - 1), 1)
            product(Lin(PAIRS - 1))
            los(Lin(PAIRS - 1))
            for j in range(KT):
                split()
                at.step()
                add_tile(j)
            last_tiles(None, None, 1)
            rms(7)
            dve.wait_ge(rbc_ready, 8)
            for j in range(KT):
                dve.scalar_tensor_tensor(h[:, j, :], h[:, j, :], col(C_LNF + j), rbc[:, :], ALU.mult, ALU.mult)\
                    .then_inc(out_ready, 1)

        @block.gpsimd
        def _(pool):
            hold = holder(xh_ready)
            pool.dma_start(onehot_sb, c_onehot).then_inc(strip_in, 16)
            pool.dma_start(rel_sb[:, :], rel_2).then_inc(strip_in, 16)
            pool.dma_start(ident[:, :], c_sq[0]).then_inc(squares_landed, 16)
            pool.dma_start(masks_sb, c_sq.rearrange("m p n -> p m n")).then_inc(masks_landed, 16)
            pool.dma_start(decay, c_decay[0:P, :]).then_inc(decay_landed, 16)
            pool.dma_start(wf_raw[:, :, :], wf).then_inc(small_in, 16)
            pool.dma_start(fb_b, f_bias.partition_broadcast(P)).then_inc(small_in, 16)
            pool.dma_start(sink_b, sinks.partition_broadcast(P)).then_inc(small_in, 16)

            def sum_squares(n):
                wait(pool, sq_ready, 8 * n + 2)
                pool.tensor_tensor(acc[:, :], sq[:, 0, :], sq[:, 1, :], ALU.add).then_inc(acc_sum, 1)
                for k in range(1, 6):
                    wait(pool, acc_sum, 6 * n + k)
                    wait(pool, sq_ready, 8 * n + k + 2)
                    pool.tensor_tensor(acc[:, :], acc[:, :], sq[:, (k + 1) % 4, :], ALU.add).then_inc(acc_sum, 1)

            sum_squares(0)
            pool.wait_ge(strip_copied, 1)
            pool.dma_start(strips, strip_sb.unsqueeze(1).broadcast_to([12, P, STRIP])).then_inc(strip_saved, 16)

            def y_los(hd):
                for c in range(4):
                    wait(pool, y_hi, hd * 4 + (c + 1))
                    pool.tensor_tensor(ry_l[c], oc[c], f32(ry_h[c]), ALU.subtract).then_inc(y_lo, 1)

            def ret_head(hd, first):
                if not first:
                    wait(pool, ret_p, hd * 4)
                    pool.dma_start(decay, c_decay[bass.ds((hd * P).val(), P), :]).then_inc(decay_landed, 16)
                    y_los(hd - 1)
                for n in range(4):
                    wait(pool, rope_hi, hd * 4 + (n + 1))
                    pool.tensor_tensor(rqk_l[n], qkf[n % 2], f32(rqk_h[n]), ALU.subtract).then_inc(rope_lo, 1)
                for j in range(TT):
                    a, w = T_AT[j], T_W[j]
                    wait(pool, ret_p_hi, hd * 4 + (j + 1))
                    pool.tensor_tensor(rp_l[:, a:a + w], pf_ret[:, a:a + w], f32(rp_h[:, a:a + w]), ALU.subtract)\
                        .then_inc(ret_p_lo, 1)
                for k, (src, ready) in enumerate(((oc, ret_o), ([sq[:, c, :] for c in range(4)], gn_sq))):
                    wait(pool, ready, hd * 4 + 2)
                    pool.tensor_tensor(acc[:, :], src[0], src[1], ALU.add).then_inc(gn_sum, 1)
                    for c in (2, 3):
                        wait(pool, ready, hd * 4 + (c + 1))
                        wait(pool, gn_sum, hd * 6 + (3 * k + c - 1))
                        pool.tensor_tensor(acc[:, :], acc[:, :], src[c], ALU.add).then_inc(gn_sum, 1)

            ret_head(Lin(0), True)
            with pool.Fori(0, RH - 1) as i:
                ret_head(Lin(1, 1, i), False)
            y_los(Lin(RH - 1))
            sum_squares(1)
            sum_squares(2)

            def normalise(sm, hd, par, window=False):
                hold(pool, (sm.rinv, hd + 1))
                for t in range(TT):
                    a, w = (CP_AT[t], CP_W[t]) if window else (P_AT[t], P_W[t])
                    pool.tensor_scalar(pf[par][:, a:a + w], pf[par][:, a:a + w], rinv[par][:, t:t + 1], 1.0,
                                       ALU.mult, ALU.mult).then_inc(sm.probs, 1)

            def toeplitz(sm, hd, table, row, offset, w):
                wait(pool, sm.biased, 4 * (hd - 1) if hd >= 2 else 0)
                src = bass.AP(table.tensor, row * P * STRIP + offset + P - 1, [[STRIP - 1, P], [1, w]])
                pool.dma_start(bias[hd % 2][:, 0:w], src).then_inc(sm.bias[hd % 2], 16)

            for hd in range(2):
                toeplitz(att, hd, rel_pad, hd, 0, S)
            for hd in range(AH):
                normalise(att, hd, hd % 2)
                if hd + 2 < AH:
                    toeplitz(att, hd + 2, rel_pad, hd + 2, 0, S)
            for n in (3, 4):
                sum_squares(n)
            pool.wait_ge(xl_ready, 32)
            pool.dma_start(tri_sb, c_tri).then_inc(tri_landed, 16)
            pool.dma_start(sel_sb, c_sel).then_inc(tri_landed, 16)
            pool.wait_ge(strip_saved, 16)

            def hyb_bias(hd):
                if hd < 4:
                    toeplitz(hyb, hd, strips, hd, 0, S)
                elif 8 <= hd < 16:
                    toeplitz(hyb, hd, strips, 4 + SINK_OF[hd - 8], 256, 2 * P)

            hyb_bias(0)
            hyb_bias(1)
            sum_squares(5)
            for hd in range(16):
                normalise(hyb, hd, hd % 2, hd >= 8)
                hyb_bias(hd + 2)
            sum_squares(6)
            sum_squares(7)


def rope_tables():
    half = RK // 2
    inv = np.exp(-np.log(10000.0) * np.arange(half) / half)
    ang = inv[:, None] * np.arange(S)[None, :]
    return np.stack([np.cos(ang), np.sin(ang)]).astype(np.float32)


def decay_tables():
    m, n = np.arange(P)[:, None], np.arange(S)[None, :]
    seen = m // CH <= n // CH
    gamma = 1.0 - 2.0 ** (-5.0 - np.arange(RH))
    tab = gamma[:, None, None] ** np.abs(n - m) * RK ** -0.5 * seen
    return tab.reshape(RH * P, S).astype(np.float32)


def square_tables():
    q, k = np.arange(P)[:, None], np.arange(P)[None, :]
    masks = [(q < CH) & (k >= CH), k > q, k <= q]
    return np.stack([np.eye(P)] + [np.where(x, NEG, 0.0) for x in masks]).astype(np.float32)


def bucket_table():
    f = np.float32
    dist = np.maximum(511 - np.arange(STRIP), 0)
    exact = BUCKETS // 2
    d = np.maximum(dist.astype(f), f(1))
    large = exact + (np.log(d / f(exact)) / f(np.log(MAX_DISTANCE / exact)) * f(BUCKETS - exact)).astype(np.int32)
    bucket = np.where(dist < exact, dist, np.minimum(large, BUCKETS - 1))
    return (np.arange(BUCKETS)[:, None] == bucket[None, :]).astype(np.float32)


def features(w, c, k=KT):
    return w[:, c].reshape(k, P, P).transpose(1, 0, 2).reshape(P, k * P)


def units(a):
    out = []

    def tile(w, at):
        u = features(w, slice(at, at + P), w.shape[0] // P)
        out.append(np.pad(u, ((0, 0), (0, UNIT - u.shape[1]))))

    def tokens(w, at):
        for kk in range(4):
            out.append(w[kk * 256:(kk + 1) * 256, at:at + S].reshape(2, P, S).transpose(1, 0, 2).reshape(P, UNIT))

    def head_out(hd):
        w = a["ret_w_out"][0][hd * RV:(hd + 1) * RV]
        for c in range(4):
            part = w[:, c * 256:(c + 1) * 256].reshape(4, P, 2, P)
            out.append(part.transpose(1, 2, 0, 3).reshape(P, UNIT))

    def mlp(n):
        for g in range(4):
            for c in range(8):
                tile(a["mlp_w1"][n], g * D + c * P)
            for c in range(8):
                tile(a["mlp_w2"][n][g * D:(g + 1) * D], c * P)

    w = a["ret_w_in"][0]
    for hd in range(RH):
        for at in (hd * RK, hd * RK + P, D + hd * RK, D + hd * RK + P):
            tile(w, at)
        tokens(w, 2 * D + hd * RV)
        if hd:
            head_out(hd - 1)
        for c in range(4):
            tile(w, 4 * D + hd * RV + c * P)
    head_out(RH - 1)
    mlp(0)
    w = a["att_w_in"][0]
    tile(w, 0)
    tile(w, D)
    tokens(w, 2 * D)
    tokens(w, 2 * D + S)
    for p in range(1, 8):
        tile(w, p * P)
        tile(w, D + p * P)
    for c in range(8):
        tile(a["att_w_out"][0], c * P)
    mlp(1)
    w = a["w_in_2"][0]
    qa, ka, va, qb, kb, vb, fb, qc, kc, vc, ga, gb, gc = np.cumsum(
        [0, 256, 256, 256, 256, 256, 256, 4, 512, 128, 128, D, D])
    pairs = [np.r_[qc + j * HEAD:qc + (j + 1) * HEAD, qc + (j + 4) * HEAD:qc + (j + 5) * HEAD] for j in range(4)]
    tile(w, qa)
    tile(w, ka)
    tokens(np.concatenate([w[:, va:va + 256], w[:, vb:vb + 256]], 1), 0)
    tile(w, vc)
    tile(w, qa + P)
    tile(w, ka + P)
    for n in range(2):
        tile(w, qb + n * P)
        tile(w, kb + n * P)
    tile(w[:, pairs[0]], 0)
    tile(w, kc)
    for j in range(1, 4):
        tile(w[:, pairs[j]], 0)
    rows = np.concatenate([pair - qc for pair in pairs])
    branches = np.concatenate([a["w_pa_2"][0], a["w_pb_2"][0], a["w_pc_2"][0][rows]], 0)
    for c in range(8):
        for g in (ga, gb, gc):
            tile(w, g + c * P)
        tile(branches, c * P)
    for c in range(8):
        tile(a["w_o_2"][0], c * P)

    def up(pairs):
        for c in pairs:
            tile(a["w_up_2"][0], c * P)
            tile(a["w_up_2"][0], FF2 + c * P)

    def down(g):
        done = sum(GROUPS[:g])
        for c in range(8):
            tile(a["w_down_2"][0][done * P:(done + GROUPS[g]) * P], c * P)

    up(range(8))
    down(0)
    up(range(8, 14))
    down(1)
    up(range(14, PAIRS))
    down(2)
    down(3)
    assert len(out) == N_UNITS
    return np.stack(out)


def columns(v):
    return np.asarray(v).reshape(-1, P).T


def kernel(**inputs):
    import concourse.bacc as bacc
    from concourse.bass_utils import run_bass_kernel_spmd

    a = {k: np.asarray(v) for k, v in inputs.items()}
    fb = 6 * 256
    arrays = {
        "stream": units(a),
        "x_t": a["x"][0].T,
        "cols": np.concatenate([columns(v) for v in (
            a["mix_norm_g"][0], a["mlp_norm_g"][0], a["mix_norm_g"][1], a["mlp_norm_g"][1], a["final_norm_g"],
            a["ln1_2"][0], a["ln2_2"][0], a["ln_f_2"], a["ret_gn_g"][0],
            a["conv_w_2"][0].reshape(-1), a["conv_b_2"][0])], 1),
        "wf": a["w_in_2"][0][:, fb:fb + 4].reshape(KT, P, 4).transpose(1, 0, 2),
        "f_bias": a["b_f_2"][0],
        "sinks": a["sinks_2"][0],
        "rel_pad": np.repeat(np.pad(a["att_rel_bias"][0], ((0, 0), (255, 65)), mode="edge")[:, None], P, axis=1),
        "rel_2": a["rel_bias_2"],
        "c_rope": rope_tables(),
        "c_decay": decay_tables(),
        "c_sq": square_tables(),
        "c_tri": (np.arange(P)[:, None] <= np.arange(S)[None, :]).astype(np.float32),
        "c_sel": np.repeat(np.eye(4), P, axis=1).astype(np.float32),
        "c_onehot": bucket_table(),
    }
    nc = bacc.Bacc("TRN2", target_bir_lowering=False, num_devices=1)
    feed, args = {}, []
    for name, v in arrays.items():
        v = np.ascontiguousarray(v)
        feed["in_" + name] = v
        args.append(nc.dram_tensor("in_" + name, v.shape, mybir.dt.from_np(v.dtype), kind="ExternalInput").ap())
    out = nc.dram_tensor("out_t", (D, S), F32, kind="ExternalOutput").ap()
    build(nc, *args, out)
    got = run_bass_kernel_spmd(nc, [feed], core_ids=[0]).results[0]["out_t"]
    return np.ascontiguousarray(got.T)[None]
```

```python
from contextlib import ExitStack

import numpy as np
import concourse.bass as bass
from concourse import mybir

F32 = mybir.dt.float32
F32R = mybir.dt.float32r
ALU = mybir.AluOpType
ACT = mybir.ActivationFunctionType

P = 128
S = 512
D = 1024
KT = D // P
TT = S // P
EPS = 1e-6
NEG = -1e30
LOWEST = -3.4028235e38
UNIT = 1024
RING = 4
LEAD = 3

RH, RK, RV, CH = 4, 256, 512, 64
AH = 16
REL_MAX, REL_TABLE = 256, 320
BUCKETS, MAX_DISTANCE = 32, 4096
HEAD, WINDOW = 64, 128
FF2 = 2816
PAIRS = FF2 // P
GROUPS = [6, 6, 6, 4]
SCALE = HEAD ** -0.5
NORMS, BOTH = 7, 4
STRIP = 640

C_MIX0, C_MLP0, C_MIX1, C_MLP1, C_FIN, C_LN1, C_LN2, C_LNF = [8 * n for n in range(8)]
C_BOTH = -1
C_GN = 64
C_CW = C_GN + RH * RV // P
C_CB = C_CW + 3 * 2 * PAIRS
N_COLS = C_CB + 2 * PAIRS

U_RET = 12 + 3 * 16 + 4
U_MLP = 64
U_ATT = 2 + 8 + 14 + 8
U_HEADS = 5 + 13
U_MERGE = 4 * KT
U_WO = KT
U_GLU = 2 * PAIRS + len(GROUPS) * KT
N_UNITS = U_RET + U_MLP + U_ATT + U_MLP + U_HEADS + U_MERGE + U_WO + U_GLU

P_AT, P_W = [0, 128, 384, 768], [128, 256, 384, 512]
T_AT, T_W = [0, 512, 896, 1152], [512, 384, 256, 128]
CP_AT, CP_W = [0, 128, 384, 640], [128, 256, 256, 256]
CT_AT, CT_W = [0, 256, 512, 768], [256, 256, 256, 128]


HYB_UNITS = {-1: (2, (1, 0)), 0: (3, (1, 1)), 1: (4, (0, 0)), 2: (5, (0, 1)), 3: (6, (1, 0)), 4: (7, (1, 1)),
             5: (8, (0, 0)), 6: (9, (0, 1)), 7: (10, (1, 0)), 9: (11, (0, 0)), 11: (12, (1, 0))}
GATE_STEPS = {8: 0, 10: 1, 12: 2, 13: 3, 14: 4, 15: 5}
HYB_TILES = [2, 4, 6, 8, 10, 11, 12, 13]
SINK_OF = [j + 4 * half for j in range(4) for half in range(2)]
BIAS_COUNT = [16, 16, 32, 32, None, None, None, None] + [48 + 16 * (n // 2) for n in range(8)]


class Lin:

    def __init__(self, b, a=0, i=None):
        self.b, self.a, self.i = b, a, i

    def __add__(self, n):
        return Lin(self.b + n, self.a, self.i)

    def __sub__(self, n):
        return self + -n

    def __mul__(self, n):
        return Lin(self.b * n, self.a * n, self.i)

    def __floordiv__(self, n):
        assert self.a % n == 0
        return Lin(self.b // n, self.a // n, self.i)

    def __mod__(self, n):
        assert self.a % n == 0
        return self.b % n

    def val(self):
        if not self.a or self.i is None:
            return self.b
        x = self.i if self.a == 1 else self.i * self.a
        return x + self.b if self.b else x

    def fold(self, m):
        return Lin(self.b % m, self.a, self.i)

    def positive(self):
        return self.b > 0 or bool(self.a)


def lin(x):
    return x if isinstance(x, Lin) else Lin(x)


def holder(sem):
    k = [0]

    def hold(eng, *waits):
        counts = [lin(count).val() for _, count in waits]
        counts = [c if isinstance(c, int) else eng.to_reg(c) for c in counts]
        if any(not isinstance(c, int) for c in counts):
            k[0] = k[0] % 16 + 1
            eng.wait_ge(sem, k[0])
        for (of, count), c in zip(waits, counts):
            assert lin(count).b > 0 or not lin(count).a
            if lin(count).positive():
                eng.wait_ge(of, c)
    return hold


class Place:

    def __init__(self):
        self.u, self.pe, self.t = Lin(0), Lin(0), Lin(0)

    def enter(self, i, du, dpe, dt):
        self.start = [self.u.b, self.pe.b, self.t.b]
        self.per = [du, dpe, dt]
        self.u, self.pe, self.t = (Lin(b, a, i) for b, a in zip(self.start, self.per))

    def leave(self, n):
        now = [self.u.b, self.pe.b, self.t.b]
        assert now == [b + a for b, a in zip(self.start, self.per)], (now, self.start, self.per)
        self.u, self.pe, self.t = (Lin(b + n * a) for b, a in zip(self.start, self.per))

    def step(self, pe=1, t=1):
        self.u, self.pe, self.t = self.u + 1, self.pe + pe, self.t + t


def wait(eng, sem, count):
    count = lin(count)
    assert count.b > 0 or not count.a, count.b
    if count.positive():
        eng.wait_ge(sem, count.val())


def build(nc, stream, x_t, cols, wf, f_bias, sinks, rel_pad, rel_2, c_rope, c_decay, c_sq, c_tri, c_sel,
          c_onehot, c_masked, out):
    strips = nc.dram_tensor("bias_strips", (12, P, STRIP), F32, kind="Internal").ap()
    with ExitStack() as ctx:
        def sb(name, shape, dt=F32):
            return ctx.enter_context(nc.sbuf_tensor(name, shape, dt))

        def sem(name):
            return ctx.enter_context(nc.semaphore(name))

        raw = sb("raw", [P, RING, UNIT])
        w_hi = sb("w_hi", [P, RING, UNIT], F32R)
        w_lo = sb("w_lo", [P, RING, UNIT], F32R)
        h = sb("h", [P, KT, S])
        x_hi = sb("x_hi", [P, KT, S], F32R)
        x_lo = sb("x_lo", [P, KT, S], F32R)
        rbc = sb("rbc", [P, S])
        sq = sb("sq", [P, 4, S])
        acc = sb("acc", [P, S])
        diag = sb("diag", [P, TT, P])
        ident = sb("ident", [P, P])
        ones = sb("ones", [P, P])
        sqr = sb("sqr", [P, 3, P], F32R)
        colv = sb("colv", [P, N_COLS])
        small = sb("small", [P, 12, 16])
        wf_raw = sb("wf_raw", [P, KT, 4])
        wf_hi = sb("wf_hi", [P, KT, 4], F32R)
        wf_lo = sb("wf_lo", [P, KT, 4], F32R)
        rel_sb = sb("rel_sb", [BUCKETS + 2, 12])
        arena = sb("arena", [P, 17 * S])
        arena_r = sb("arena_r", [P, 29 * S], F32R)

        banks = [ctx.enter_context(nc.psum_tensor(f"bank{n}", [P, S], F32)) for n in range(8)]

        def f_at(tile, n=1):
            return arena[:, tile * S:(tile + n) * S]

        def r_at(tile, n=1):
            return arena_r[:, tile * S:(tile + n) * S]

        def f32(ap):
            return ap.bitcast(F32)

        def col(n):
            n = lin(n)
            return colv[:, n.b:n.b + 1] if not n.a else colv[:, bass.ds(n.val(), 1)]

        ms, sd, rcol = small[:, 0, 0:4], small[:, 1, 0:4], small[:, 2, 0:4]
        gn_ms, gn_sd, gn_r = small[:, 0, 4:8], small[:, 1, 4:8], small[:, 2, 4:8]
        mx = [small[:, 3, 4 * n:4 * n + 4] for n in range(2)]
        nm = [small[:, 4, 4 * n:4 * n + 4] for n in range(2)]
        sums = [small[:, 5, 4 * n:4 * n + 4] for n in range(2)]
        rinv = [small[:, 6, 4 * n:4 * n + 4] for n in range(2)]
        es = [small[:, 3, 8 + 4 * n:12 + 4 * n] for n in range(2)]
        sink_b, nsink = small[:, 7, 0:8], small[:, 7, 8:16]
        fb_b = small[:, 6, 8:12]
        gains_2 = small[:, 5, 8:16]
        ms_2, sd_2 = small[:, 0, 8:16], small[:, 1, 8:16]
        m2, r_first = small[:, 2, 8:12], small[:, 2, 12:16]
        fl, fe, fn = small[:, 8, :], small[:, 9, :], small[:, 10, :]
        flog = small[:, 11, :]
        sums2 = [small[:, 4, 8 + 4 * n:12 + 4 * n] for n in range(2)]

        x_landed = [sem(f"x_landed{j}") for j in range(KT)]
        cols_landed = sem("cols_landed")
        squares_landed = sem("squares_landed")
        masks_landed = sem("masks_landed")
        masks_ready = sem("masks_ready")
        rope_landed = sem("rope_landed")
        strip_in = sem("strip_in")
        small_in = sem("small_in")
        strip_made = sem("strip_made")
        strip_copied = sem("strip_copied")
        strip_saved = sem("strip_saved")
        consts_made = sem("consts_made")
        raw_landed = [sem(f"raw_landed{n}") for n in range(RING)]
        hi_ready = sem("hi_ready")
        lo_ready = sem("lo_ready")
        products_done = sem("products_done")
        tile_read = sem("tile_read")
        xh_ready = sem("xh_ready")
        xl_ready = sem("xl_ready")
        sq_ready = sem("sq_ready")
        acc_sum = sem("acc_sum")
        stat_done = sem("stat_done")
        ms_ready = sem("ms_ready")
        sd_ready = sem("sd_ready")
        rcol_ready = sem("rcol_ready")
        diag_ready = sem("diag_ready")
        rbc_ready = sem("rbc_ready")
        gains_made = sem("gains_made")
        sq2_ready = sem("sq2_ready")
        sum2 = sem("sum2")
        ms_part = sem("ms_part")
        r_first_ready = sem("r_first_ready")
        first_diag = sem("first_diag")
        first_spread = sem("first_spread")
        h_normed = sem("h_normed")
        rope_tables = sem("rope_tables")
        rope_ready = sem("rope_ready")
        rope_hi = sem("rope_hi")
        rope_lo = sem("rope_lo")
        v_hi = sem("v_hi")
        v_lo = sem("v_lo")
        decay_landed = sem("decay_landed")
        ret_scores = sem("ret_scores")
        ret_p = sem("ret_p")
        ret_p_hi = sem("ret_p_hi")
        ret_p_lo = sem("ret_p_lo")
        ret_pv = sem("ret_pv")
        ret_o = sem("ret_o")
        gn_sum = sem("gn_sum")
        gn_done = sem("gn_done")
        gn_centred = sem("gn_centred")
        gn_sq = sem("gn_sq")
        gn_ms_r = sem("gn_ms_r")
        gn_sd_r = sem("gn_sd_r")
        gn_r_r = sem("gn_r_r")
        gn_diag = sem("gn_diag")
        gate_ready = sem("gate_ready")
        y_scaled = sem("y_scaled")
        y_ready = sem("y_ready")
        y_hi = sem("y_hi")
        y_lo = sem("y_lo")
        u_ready = sem("u_ready")
        u_hi = sem("u_hi")
        u_lo = sem("u_lo")

        class Heads:

            def __init__(self, n):
                self.scores = sem(f"{n}_scores")
                self.biased = sem(f"{n}_biased")
                self.negmax = sem(f"{n}_negmax")
                self.exp = sem(f"{n}_exp")
                self.rinv = sem(f"{n}_rinv")
                self.probs = sem(f"{n}_probs")
                self.turned = sem(f"{n}_turned")
                self.turned_hi = sem(f"{n}_turned_hi")
                self.turned_lo = sem(f"{n}_turned_lo")
                self.pv = sem(f"{n}_pv")
                self.o = sem(f"{n}_o")
                self.qk_hi = sem(f"{n}_qk_hi")
                self.qk_lo = sem(f"{n}_qk_lo")
                self.bias = [sem(f"{n}_bias0"), sem(f"{n}_bias1")]

        att = Heads("att")
        hyb = Heads("hyb")
        att_v = sem("att_v")
        bias_masked = sem("bias_masked")
        stage_hi = sem("stage_hi")
        stage_lo = sem("stage_lo")
        hyb_vh = sem("hyb_vh")
        hyb_vl = sem("hyb_vl")
        hc_turned = sem("hc_turned")
        wf_h = sem("wf_h")
        wf_l = sem("wf_l")
        tri_landed = sem("tri_landed")
        f_done = sem("f_done")
        f_row_ready = sem("f_row_ready")
        f_step = sem("f_step")
        f_act = sem("f_act")
        cum_done = sem("cum_done")
        cum_row = sem("cum_row")
        cum_bc = sem("cum_bc")
        cum_bias = sem("cum_bias")
        sink_ready = sem("sink_ready")
        sink_exp = sem("sink_exp")
        sink_sum = sem("sink_sum")
        o_hi = sem("o_hi")
        o_lo = sem("o_lo")
        gate_read = sem("gate_read")
        gate_sig = sem("gate_sig")
        branch_read = sem("branch_read")
        merge_a = sem("merge_a")
        merged = sem("merged")
        pad_made = sem("pad_made")
        conv_0 = sem("conv_0")
        conv_1 = sem("conv_1")
        conv_2 = sem("conv_2")
        silu_done = sem("silu_done")
        s_ready = sem("s_ready")
        s_hi = sem("s_hi")
        s_lo = sem("s_lo")
        out_ready = sem("out_ready")
        stored = sem("stored")

        cosr, sinr = f_at(0), f_at(1)
        rt = [f_at(2 + n) for n in range(4)]
        qkf = [f_at(6), f_at(7)]
        pf_ret = f_at(2, 3)
        oc = [f_at(8 + n) for n in range(4)]
        sg = [f_at(12 + n) for n in range(4)]
        decay = f_at(16)
        rqk_h = [r_at(n) for n in range(4)]
        rqk_l = [r_at(4 + n) for n in range(4)]
        rv_h = [r_at(8 + n) for n in range(4)]
        rv_l = [r_at(12 + n) for n in range(4)]
        rp_h, rp_l = arena_r[:, 16 * S:16 * S + 1280], arena_r[:, 16 * S + 1280:16 * S + 2560]
        ry_h = [r_at(21 + n) for n in range(4)]
        ry_l = [r_at(25 + n) for n in range(4)]
        onehot_sb = arena[0:BUCKETS + 2, 8 * S:8 * S + STRIP]
        strip_sb = arena[0:12, 10 * S:10 * S + STRIP]
        masks_sb = arena[:, 12 * S:12 * S + 3 * P].rearrange("p (m n) -> p m n", m=3)
        zf = [f_at(0), f_at(1)]
        uf = [f_at(2), f_at(3)]
        uh = [r_at(n) for n in range(KT)]
        ul = [r_at(8 + n) for n in range(KT)]
        pf = [arena[:, n * 1280:(n + 1) * 1280] for n in range(2)]
        af = [f_at(5), f_at(6)]
        bias = [f_at(7), f_at(8)]
        vf = arena[:, 9 * S:17 * S].rearrange("p (a t d) -> p a t d", a=8, t=TT)
        of = [f_at(9 + n) for n in range(KT)]
        sq2 = [f_at(9 + n) for n in range(4)]
        acc2 = f_at(13)

        def pair_tile(pair, a=0, b=P):
            if not pair.a:
                return arena[a:b, (9 + pair.b) * S:(10 + pair.b) * S]
            return arena[a:b, bass.ds((pair * S + 9 * S).val(), S)]

        def mf_at(c):
            return mf[:, c.b, :] if not c.a else arena[:, bass.ds((c * S + 9 * S).val(), S)]

        ah = [[r_at(2 * n + m) for m in range(2)] for n in range(2)]
        al = [[r_at(4 + 2 * n + m) for m in range(2)] for n in range(2)]
        pt_h, pt_l = arena_r[:, 8 * S:8 * S + 1280], arena_r[:, 8 * S + 1280:8 * S + 2560]
        vs_h, vs_l = r_at(13), r_at(14)
        ao_h = [r_at(15 + n) for n in range(KT)]
        ao_l = [r_at(23 + n) for n in range(6)] + [r_at(n) for n in range(2)]
        hv_h = [r_at(13 + n) for n in range(4)]
        hv_l = [r_at(17 + n) for n in range(4)]
        hc_f = f_at(6)
        hc_h, hc_l = r_at(21), r_at(22)
        f_row = arena[0:4, 13 * S:14 * S]
        tri_sb, cum_sb, sel_sb = f_at(16), arena[0:4, 15 * S:16 * S], arena[0:4, 14 * S:15 * S]
        oh = [r_at(n) for n in range(KT)]
        ol = [r_at(8 + n) for n in range(KT)]
        gf = [f_at(n) for n in range(3)]
        gate_0 = [sq[:, n, :] for n in range(4)] + [acc[:, :], diag[:, :, :].rearrange("p t n -> p (t n)")]
        mt = [f_at(3 + n) for n in range(4)]
        mf = arena[:, 9 * S:17 * S].rearrange("p (c n) -> p c n", c=KT)
        mg_h = [r_at(16 + n) for n in range(KT)]
        mg_l = [r_at(24 + n) for n in range(5)] + [r_at(n) for n in range(3)]
        cz = [arena[:, n * 520:n * 520 + S + 2] for n in range(4)]
        cy = [f_at(5 + n) for n in range(4)]
        sf = [f_at(9), f_at(10)]
        sh_all = arena_r[:, 0:12 * S].rearrange("p (c n) -> p c n", c=12)
        sl_all = arena_r[:, 12 * S:24 * S].rearrange("p (c n) -> p c n", c=12)

        block = ctx.enter_context(nc.Block())

        @block.sync
        def _(sp):
            flat = stream.rearrange("u p n -> (u p) n")
            for u in range(RING):
                if u:
                    sp.wait_ge(x_landed[2 * u - 1], 16)
                sp.dma_start(raw[:, u, :], flat[u * P:(u + 1) * P, :]).then_inc(raw_landed[u], 16)
            with sp.Fori(0, N_UNITS // RING - 1) as i:
                for j in range(RING):
                    u = Lin(RING + j, RING, i)
                    wait(sp, lo_ready, u - (RING - 1))
                    sp.dma_start(raw[:, j, :], flat[bass.ds((u * P).val(), P), :]).then_inc(raw_landed[j], 16)
            for u in range(N_UNITS // RING * RING, N_UNITS):
                wait(sp, lo_ready, u - (RING - 1))
                sp.dma_start(raw[:, u % RING, :], flat[u * P:(u + 1) * P, :]).then_inc(raw_landed[u % RING], 16)
            for j in range(KT):
                wait(sp, out_ready, j + 1)
                sp.dma_start(out[j * P:(j + 1) * P, :], h[:, j, :]).then_inc(stored, 16)
            sp.wait_ge(stored, 16 * KT)

        @block.tensor
        def _(pe):
            at = Place()

            def mm3(dst, left, right, start, stop, check=True):
                (lh, ll), (rh, rl) = left, right
                kw = {} if check else {"skip_group_check": True}
                pe.matmul(dst, lh, rh, start=start, stop=False, **kw)
                pe.matmul(dst, lh, rl, start=False, stop=False, **kw)
                return pe.matmul(dst, ll, rh, start=False, stop=stop, **kw)

            def xs(k):
                return x_hi[:, k, :], x_lo[:, k, :]

            def w_at(slot, a, b):
                return w_hi[:, slot, a:b], w_lo[:, slot, a:b]

            def proj(src=xs, n=KT, first=None, hooks={}, bank=None):
                slot = at.u % RING
                wait(pe, lo_ready, at.u + 1)
                rotating = bank is None
                if rotating:
                    bank = banks[at.t % 2]
                    wait(pe, tile_read, at.t - 1)
                for k in range(n):
                    if k in hooks:
                        hooks[k]()
                    if first:
                        for s, base in first:
                            wait(pe, s, lin(base) + (k + 1))
                    m = mm3(bank[:, :], w_at(slot, k * P, k * P + P), src(k), k == 0, k == n - 1)
                m.then_inc(products_done, 1)
                at.step(1, 1 if rotating else 0)

            def token_major(kk, hooks={}, banks_read=None):
                slot = at.u % RING
                wait(pe, lo_ready, at.u + 1)
                for k in range(2):
                    if k in hooks:
                        hooks[k]()
                    for t in range(TT):
                        if banks_read and k == 0:
                            wait(pe, banks_read[0], banks_read[1] + t + 1)
                        xk = (x_hi[:, 2 * kk + k, t * P:t * P + P], x_lo[:, 2 * kk + k, t * P:t * P + P])
                        m = mm3(banks[4 + t][:, :], xk, w_at(slot, k * S, k * S + S),
                                kk == 0 and k == 0, kk == 3 and k == 1)
                m.then_inc(products_done, 1)
                at.step(1, 0)

            def mean_square(n):
                wait(pe, acc_sum, 6 * (n + 1))
                wait(pe, sq_ready, 8 * (n + 1))
                wait(pe, consts_made, 1)
                for t in range(TT):
                    pe.matmul(banks[2][:, t:t + 1], acc[:, t * P:t * P + P], ones[:, 0:1], start=True, stop=False)
                    m = pe.matmul(banks[2][:, t:t + 1], sq[:, 3, t * P:t * P + P], ones[:, 0:1],
                                  start=False, stop=True)
                if n == BOTH:
                    wait(pe, sum2, 7)
                    for t in range(TT):
                        m = pe.matmul(banks[2][:, 4 + t:5 + t], acc2[:, t * P:t * P + P], ones[:, 0:1],
                                      start=True, stop=True)
                m.then_inc(stat_done, 1)

            def spread_rms(n):
                wait(pe, diag_ready, n + 1)
                pe.matmul(banks[3][:, :], ones[:, :], diag[:, :, :], start=True, stop=True).then_inc(stat_done, 1)

            pe.wait_ge(strip_in, 48)
            pe.matmul(banks[6][0:12, 0:512], rel_sb[:, :], onehot_sb[:, 0:512], start=True, stop=True)
            pe.matmul(banks[7][0:12, 0:128], rel_sb[:, :], onehot_sb[:, 512:640], start=True, stop=True)\
                .then_inc(strip_made, 1)

            def gn_spread(hd):
                wait(pe, gn_diag, hd + 1)
                pe.matmul(banks[2][:, :], ones[:, :], diag[:, :, :], start=True, stop=True).then_inc(gn_done, 1)

            def two_tiles(src, first=None):
                slot = at.u % RING
                wait(pe, lo_ready, at.u + 1)
                for c in range(2):
                    wait(pe, tile_read, at.t - 1)
                    for k in range(4):
                        if first and c == 0:
                            wait(pe, first[0], first[1] + (k + 1))
                        m = mm3(banks[at.t % 2][:, :], w_at(slot, (4 * c + k) * P, (4 * c + k + 1) * P),
                                src(k), k == 0, k == 3)
                    m.then_inc(products_done, 1)
                    at.pe, at.t = at.pe + 1, at.t + 1
                at.u = at.u + 1

            def ret_out(ready=None):
                for n in range(4):
                    two_tiles(lambda k: (ry_h[k], ry_l[k]), (y_lo, ready) if ready and n == 0 else None)

            def ret_head(hd, first):
                if first:
                    proj(first=[(xl_ready, 0)], hooks={7: lambda: mean_square(0)})
                    proj(hooks={4: lambda: spread_rms(0)})
                else:
                    proj(hooks={5: lambda: gn_spread(hd - 1)})
                    proj()
                proj()
                proj()
                if first:
                    pe.wait_ge(strip_copied, 1)
                wait(pe, ret_o, hd * 4)
                for kk in range(4):
                    token_major(kk)
                if not first:
                    wait(pe, y_lo, hd * 4)
                    ret_out()
                wait(pe, rope_lo, hd * 4 + 4)
                for j, (b, o) in enumerate([(2, 0), (3, 0), (4, 0), (4, 256)]):
                    if j == 2:
                        wait(pe, v_lo, hd * 4 + 4)
                    for d in range(2):
                        keys = (rqk_h[2 + d][:, j * P:j * P + P], rqk_l[2 + d][:, j * P:j * P + P])
                        m = mm3(banks[b][:, o:o + T_W[j]], keys, (rqk_h[d][:, j * P:S], rqk_l[d][:, j * P:S]),
                                d == 0, d == 1)
                    m.then_inc(ret_scores, 1)
                proj()
                wait(pe, ret_p_lo, hd * 4 + 4)
                for c in range(4):
                    for j in range(TT):
                        val = (rv_h[j][:, c * P:c * P + P], rv_l[j][:, c * P:c * P + P])
                        sc = (rp_h[:, T_AT[j]:T_AT[j] + T_W[j]], rp_l[:, T_AT[j]:T_AT[j] + T_W[j]])
                        m = mm3(banks[4 + c][:, j * P:S], val, sc, j == 0, j == TT - 1)
                    m.then_inc(ret_pv, 1)
                proj()

                def mean():
                    wait(pe, gn_sum, hd * 6 + 3)
                    pe.matmul(banks[2][:, :], ones[:, :], acc[:, :], start=True, stop=True).then_inc(gn_done, 1)

                def variance():
                    wait(pe, gn_sum, hd * 6 + 6)
                    for t in range(TT):
                        m = pe.matmul(banks[3][:, t:t + 1], acc[:, t * P:t * P + P], ones[:, 0:1],
                                      start=True, stop=True)
                    m.then_inc(gn_done, 1)

                proj(hooks={3: mean})
                proj(hooks={6: variance})

            ret_head(Lin(0), True)
            with pe.Fori(0, RH - 1) as i:
                at.enter(i, 16, 20, 16)
                ret_head(Lin(1, 1, i), False)
                at.leave(RH - 1)
            gn_spread(Lin(RH - 1))
            ret_out(4 * (RH - 1))

            def us(k):
                return uh[k], ul[k]

            def mlp(q, n, base):
                proj(first=[(xl_ready, 8 * q)], hooks={7: lambda: mean_square(n)})
                proj(hooks={4: lambda: spread_rms(n)})
                for _ in range(6):
                    proj()
                with pe.Fori(0, 3) as i:
                    at.enter(i, 16, 16, 16)
                    proj(us, first=[(u_lo, Lin(base, 8, i))])
                    for _ in range(7):
                        proj(us)
                    for _ in range(8):
                        proj()
                    at.leave(3)
                proj(us, first=[(u_lo, base + 24)])
                for _ in range(7):
                    proj(us)

            mlp(1, 1, 0)

            def scores(sm, hd, q, k, half, kind):
                lo, hi = HEAD * half, HEAD * half + HEAD
                if kind == "window":
                    places = [(2, 0), (2, 128), (3, 0), (3, 256)]
                else:
                    places = [(2, 0), (4, 0), (2, 128), (3, 0)]
                for t, (b, o) in enumerate(places):
                    w = (CP_W if kind == "window" else P_W)[t]
                    k0 = (t + 1) * P - w
                    dst = banks[b][:, o:o + w]
                    m = mm3(dst, (q[0][lo:hi, t * P:t * P + P], q[1][lo:hi, t * P:t * P + P]),
                        (k[0][lo:hi, k0:k0 + w], k[1][lo:hi, k0:k0 + w]), True, kind != "key", False)
                    if kind == "key":
                        m = pe.matmul(dst[:, w - P:w], sqr[:, 0, :], sqr[:, 2, :],
                                      start=False, stop=True, skip_group_check=True)
                m.then_inc(sm.scores, 1)

            def turn(sm, hd, par, kind):
                window = kind == "window"
                wait(pe, sm.probs, hd * 4 + 4)
                wait(pe, sm.o, hd)
                places = [(5, 0), (5, 256), (6, 0), (6, 256)] if window else [(5, 0), (6, 0), (7, 0), (6, 384)]
                for j, (b, o) in enumerate(places):
                    for t in range(j, min(j + 2, TT) if window else TT):
                        k0 = 0 if not window else (t + 1) * P - CP_W[t]
                        src = (CP_AT if window else P_AT)[t] + j * P - k0
                        m = pe.transpose(banks[b][:, o + (t - j) * P:o + (t - j) * P + P],
                                         pf[par][:, src:src + P], ident[:, :])
                m.then_inc(sm.turned, 1)

            def weigh(sm, hd, values, kind):
                window = kind == "window"
                ta, tw = (CT_AT, CT_W) if window else (T_AT, T_W)
                wait(pe, sm.turned_lo, hd * 4 + 4)
                for j in range(TT):
                    m = mm3(banks[7][:, j * P:j * P + tw[j]], values(j),
                            (pt_h[:, ta[j]:ta[j] + tw[j]], pt_l[:, ta[j]:ta[j] + tw[j]]),
                            j == 0, j == TT - 1, False)
                m.then_inc(sm.pv, 1)

            def staged(j):
                return vs_h[:, j * P:j * P + P], vs_l[:, j * P:j * P + P]

            def attended(k):
                return ao_h[k], ao_l[k]

            def att_step(s, par, unit=True, late=True, early=True, half=None):
                head_par, pair_par = par
                if late:
                    turn(att, s - 1, head_par, "chunk")
                if unit:
                    proj()
                if half is not None:
                    two_tiles(attended, (xl_ready, 24) if half == 0 else None)
                if late:
                    if head_par == 0:
                        wait(pe, stage_lo, (s + 1) // 2)
                    weigh(att, s - 1, staged, "chunk")
                if early:
                    wait(pe, att.qk_lo, s + (3 - head_par))
                    wait(pe, att.biased, (s + 1) * 4)
                    if s.b == -1:
                        pe.wait_ge(masks_ready, 1)
                        pe.wait_ge(squares_landed, 16)
                        pe.wait_ge(att_v, 8)
                    k_of = (ah[pair_par][1], al[pair_par][1])
                    scores(att, s + 1, (ah[pair_par][0], al[pair_par][0]), k_of, head_par, "chunk")

            proj(first=[(xl_ready, 16)], hooks={7: lambda: mean_square(2)})
            proj(hooks={4: lambda: spread_rms(2)})
            for c in range(2):
                for kk in range(4):
                    token_major(kk, banks_read=(att_v, 0) if c and kk == 0 else None)
            att_step(Lin(-1), (0, 0), late=False)
            att_step(Lin(0), (1, 0), late=False)
            for j in range(4):
                att_step(Lin(1 + j), (j % 2, (1 + j // 2) % 2))
            with pe.Fori(0, 2) as i:
                at.enter(i, 4, 4, 4)
                for j in range(4):
                    att_step(Lin(5 + j, 4, i), (j % 2, (1 + j // 2) % 2))
                at.leave(2)
            for s in range(13, 17):
                att_step(Lin(s), ((s + 1) % 2, (s + 1) // 2 % 2), unit=False, early=s < 15, half=s - 13)
            for n in range(4):
                two_tiles(lambda k: attended(4 + k), (xl_ready, 28) if n == 0 else None)

            mlp(4, 3, 32)

            def spread_first():
                wait(pe, first_diag, 1)
                pe.matmul(banks[3][:, :], ones[:, :], diag[:, :, :], start=True, stop=True).then_inc(first_spread, 1)

            proj(first=[(xl_ready, 40)], hooks={7: lambda: mean_square(BOTH)})
            proj(hooks={4: lambda: spread_rms(BOTH)})
            for kk in range(4):
                token_major(kk, {0: spread_first} if kk == 1 else {})
            proj()
            pe.wait_ge(wf_l, 1)
            for k in range(KT):
                m = mm3(banks[2][0:4, :], (wf_hi[:, k, :], wf_lo[:, k, :]), (x_hi[:, k, :], x_lo[:, k, :]),
                        k == 0, k == KT - 1)
            m.then_inc(f_done, 1)
            wait(pe, tile_read, at.t)
            pe.wait_ge(h_normed, KT)
            for t in range(TT):
                m = pe.transpose(banks[3][:, t * P:t * P + P], hc_f[:, t * P:t * P + P], ident[:, :])
            m.then_inc(hc_turned, 1)

            def hyb_values(p):
                if p < 4:
                    return lambda j: (hv_h[j][:, p * P:p * P + P], hv_l[j][:, p * P:p * P + P])
                return lambda j: (hc_h[:, j * P:j * P + P], hc_l[:, j * P:j * P + P])

            for s in range(-1, 17):
                if 4 <= s < 8:
                    pe.wait_ge(cum_bias, s - 3)
                if s == 1:
                    pe.wait_ge(cum_row, 1)
                if s >= 1:
                    hd = s - 1
                    turn(hyb, Lin(hd), hd % 2, "causal" if hd < 8 else "window")
                if s in HYB_UNITS or s in GATE_STEPS:
                    proj()
                if s == -1:
                    pe.wait_ge(f_row_ready, 1)
                    for t in range(TT):
                        m = pe.transpose(banks[6][:, 4 * t:4 * t + 4], f_row[:, t * P:t * P + P], ident[0:4, 0:4])
                    m.then_inc(f_done, 1)
                if s >= 1:
                    weigh(hyb, Lin(hd), hyb_values(hd // 2), "causal" if hd < 8 else "window")
                if 4 <= s + 1 < 8:
                    wait(pe, hyb.turned_lo, 4 * s)
                    pe.matmul(banks[5][:, :], sel_sb[:, (s - 3) * P:(s - 2) * P], cum_sb[:, :],
                              start=True, stop=True).then_inc(cum_bc, 1)
                if s < 15:
                    hd = s + 1
                    p = hd // 2
                    wait(pe, hyb.qk_lo, HYB_TILES[p])
                    wait(pe, hyb.biased, 4 * hd)
                    if hd == 0:
                        pe.wait_ge(hyb_vl, 5)
                    kp = p % 2 if p < 4 else 0
                    scores(hyb, hd, (ah[p % 2][0], al[p % 2][0]), (ah[kp][1], al[kp][1]), hd % 2,
                           "relative" if hd < 4 else "key" if hd < 8 else "window")
                if s == 0:
                    pe.wait_ge(f_step, 5)
                    pe.wait_ge(tri_landed, 32)
                    for t in range(TT):
                        m = pe.matmul(banks[5][0:4, t * P:S], flog[:, 4 * t:4 * t + 4], tri_sb[:, 0:S - t * P],
                                      start=(t == 0), stop=(t == TT - 1))
                    m.then_inc(cum_done, 1)

            wait(pe, tile_read, at.t)

            def gates(c):
                for g, b in enumerate((0, 1, 5)):
                    wait(pe, gate_read, c * 3 + (g - 2) if c.a else 0)
                    proj(bank=banks[b])

            def branches(c):
                slot = at.u % RING
                wait(pe, lo_ready, at.u + 1)
                wait(pe, o_lo, 8)
                for g, (a, b) in enumerate(((0, 2), (2, 4), (4, 8))):
                    wait(pe, branch_read, c * 3 + (g - 2) if c.a or c.b else 0)
                    for k in range(a, b):
                        m = mm3(banks[2 + g][:, :], w_at(slot, k * P, k * P + P), (oh[k], ol[k]), k == a, k == b - 1)
                m.then_inc(products_done, 1)
                at.step(1, 0)

            gates(Lin(0))
            for c in range(3):
                branches(Lin(c))
            with pe.Fori(0, 5) as i:
                at.enter(i, 4, 4, 0)
                gates(Lin(1, 1, i))
                branches(Lin(3, 1, i))
                at.leave(5)
            pe.wait_ge(gate_read, 3 * (KT - 2))
            def merged_at(k):
                return mg_h[k], mg_l[k]

            proj(merged_at, first=[(xl_ready, 48)])
            for _ in range(7):
                proj(merged_at)

            def down(g):
                first_pair = sum(GROUPS[:g])

                def ss(k):
                    return sh_all[:, (first_pair + k - 1) % 12, :], sl_all[:, (first_pair + k - 1) % 12, :]

                proj(ss, GROUPS[g], first=[(s_lo, first_pair)])
                for _ in range(7):
                    proj(ss, GROUPS[g])

            proj(first=[(xl_ready, 56)], hooks={7: lambda: mean_square(5)})
            proj(hooks={4: lambda: spread_rms(5)})
            proj()
            proj()
            for g in range(3):
                with pe.Fori(0, 3) as i:
                    at.enter(i, 4, 4, 4)
                    for _ in range(4):
                        proj()
                    at.leave(3)
                if g < 2:
                    down(g)
            for _ in range(4):
                proj()
            down(2)
            down(3)
            assert at.u.b == N_UNITS
            mean_square(6)
            spread_rms(6)

        @block.scalar
        def _(act):
            hold = holder(xh_ready)
            at = Place()

            next_split_made = [False]

            def split(ahead=LEAD):
                if next_split_made[0]:
                    next_split_made[0] = False
                    return
                u = at.u + ahead
                if u.a == 0 and u.b >= N_UNITS:
                    return
                wait(act, raw_landed[u % RING], (u // RING + 1) * 16)
                wait(act, products_done, at.pe)
                act.activation(w_hi[:, u % RING, :], raw[:, u % RING, :], ACT.Copy).then_inc(hi_ready, 1)

            def gain_of(gain, j):
                return gains_2[:, j:j + 1] if gain == C_BOTH else col(gain + j)

            def hi_and_square(q, n, j, gain, ready, count):
                wait(act, ready, count)
                act.activation(x_hi[:, j, :], h[:, j, :], ACT.Copy, scale=gain_of(gain, j)).then_inc(xh_ready, 1)
                if j >= 4:
                    wait(act, acc_sum, 6 * n + max(1, j - 4))
                act.activation(sq[:, j % 4, :], h[:, j, :], ACT.Square).then_inc(sq_ready, 1)
                if n == BOTH:
                    if j >= 4:
                        wait(act, sum2, max(1, j - 4))
                    act.activation(sq2[j % 4], h[:, j, :], ACT.Square, scale=col(C_FIN + j)).then_inc(sq2_ready, 1)

            def square_only(n, j, ready, count):
                wait(act, ready, count)
                if j >= 4:
                    wait(act, acc_sum, 6 * n + max(1, j - 4))
                act.activation(sq[:, j % 4, :], h[:, j, :], ACT.Square).then_inc(sq_ready, 1)

            def root(n):
                if 0 < n < NORMS - 1:
                    split()
                    next_split_made[0] = True
                wait(act, ms_ready, n + 1)
                if n == BOTH:
                    act.activation(sd_2, ms_2, ACT.Sqrt).then_inc(sd_ready, 1)
                else:
                    act.activation(sd, ms, ACT.Sqrt).then_inc(sd_ready, 1)

            def keep_rms(n):
                wait(act, stat_done, 2 * n + 2)
                act.activation(rbc[:, :], banks[3][:, :], ACT.Copy).then_inc(rbc_ready, 1)

            for j in range(KT):
                act.dma_start(h[:, j, :], x_t[j * P:(j + 1) * P, :]).then_inc(x_landed[j], 16)
                if j == 0:
                    act.dma_start(colv[:, :], cols).then_inc(cols_landed, 16)
            act.dma_start(cosr, c_rope[0]).then_inc(rope_landed, 16)
            act.dma_start(sinr, c_rope[1]).then_inc(rope_landed, 16)
            act.wait_ge(cols_landed, 16)
            hi_and_square(0, 0, 0, C_MIX0, x_landed[0], 16)
            split(0)
            for j in range(1, KT):
                hi_and_square(0, 0, j, C_MIX0, x_landed[j], 16)
                if j in (4, 6):
                    split(j // 2 - 1)
            act.wait_ge(masks_landed, 16)
            act.activation(sqr[:, :, :], masks_sb, ACT.Copy).then_inc(masks_ready, 1)

            def rope_his(hd, x):
                for c in range(2):
                    wait(act, rope_ready, hd * 4 + (2 * x + c + 1))
                    act.activation(rqk_h[2 * x + c], qkf[c], ACT.Copy).then_inc(rope_hi, 1)

            def y_his(hd):
                for c in range(4):
                    wait(act, y_ready, hd * 4 + (c + 1))
                    act.activation(ry_h[c], oc[c], ACT.Copy).then_inc(y_hi, 1)

            def gate(hd, c):
                wait(act, tile_read, at.t)
                act.activation(sg[c], sg[c], ACT.Silu).then_inc(gate_ready, 1)

            def ret_head(hd, first):
                split()
                if first:
                    root(0)
                    keep_rms(0)
                at.step()
                split()
                if not first:
                    y_his(hd - 1)
                at.step()
                rope_his(hd, 0)
                split()
                at.step()
                split()
                at.step()
                rope_his(hd, 1)
                for kk in range(4):
                    split()
                    at.step(1, 0)
                wait(act, products_done, at.pe)
                for t in range(TT):
                    act.activation(rv_h[t], banks[4 + t][:, :], ACT.Copy, scale=rcol[:, t:t + 1]).then_inc(v_hi, 1)
                if not first:
                    for _ in range(4):
                        split()
                        at.step(2, 2)
                split()
                for j in range(4):
                    wait(act, ret_p, hd * 4 + (j + 1))
                    act.activation(rp_h[:, T_AT[j]:T_AT[j] + T_W[j]], pf_ret[:, T_AT[j]:T_AT[j] + T_W[j]],
                                   ACT.Copy).then_inc(ret_p_hi, 1)
                at.step()
                gate(hd, 0)
                split()
                if first:
                    act.wait_ge(strip_saved, 16)
                for c in range(4):
                    wait(act, ret_pv, hd * 4 + (c + 1))
                    act.activation(oc[c], banks[4 + c][:, :], ACT.Copy).then_inc(ret_o, 1)
                at.step()
                gate(hd, 1)
                split()
                for c in range(4):
                    wait(act, gn_centred, hd * 4 + (c + 1))
                    act.activation(sq[:, c, :], oc[c], ACT.Square).then_inc(gn_sq, 1)
                at.step()
                gate(hd, 2)
                split()
                at.step()
                wait(act, gn_ms_r, hd + 1)
                act.activation(gn_sd, gn_ms, ACT.Sqrt).then_inc(gn_sd_r, 1)
                gate(hd, 3)

            ret_head(Lin(0), True)
            with act.Fori(0, RH - 1) as i:
                at.enter(i, 16, 20, 16)
                ret_head(Lin(1, 1, i), False)
                at.leave(RH - 1)
            split()
            next_split_made[0] = True
            y_his(Lin(RH - 1))

            def last_tiles(q, n, gain, per_unit, final=False):
                for j in range(KT):
                    if j % per_unit == 0:
                        split()
                        at.u = at.u + 1
                    at.pe, at.t = at.pe + 1, at.t + 1
                    if final:
                        square_only(n, j, tile_read, at.t)
                    else:
                        hi_and_square(q, n, j, gain, tile_read, at.t)

            last_tiles(1, 1, C_MLP0, 2)

            def mlp_up(base):
                for j in range(KT):
                    split()
                    at.step()
                    wait(act, u_ready, lin(base) + (j + 1))
                    act.activation(uh[j], uf[j % 2], ACT.Copy).then_inc(u_hi, 1)

            def mlp(n, base):
                root(n)
                keep_rms(n)
                mlp_up(base)
                with act.Fori(0, 3) as i:
                    at.enter(i, 16, 16, 16)
                    for j in range(KT):
                        split()
                        at.step()
                    mlp_up(Lin(base + 8, 8, i))
                    at.leave(3)

            mlp(1, 0)
            last_tiles(2, 2, C_MIX1, 1)

            def exps(sm, hd, par, window=False):
                hold(act, (sm.negmax, hd + 1))
                for t in range(TT):
                    a, w = (CP_AT[t], CP_W[t]) if window else (P_AT[t], P_W[t])
                    act.activation(pf[par][:, a:a + w], pf[par][:, a:a + w], ACT.Exp, bias=nm[par][:, t:t + 1],
                                   accum_out=sums[par][:, t:t + 1]).then_inc(sm.exp, 1)

            def turned_his(sm, hd, window=False):
                wait(act, sm.turned, hd + 1)
                places = [(5, 0), (5, 256), (6, 0), (6, 256)] if window else [(5, 0), (6, 0), (7, 0), (6, 384)]
                for j, (b, o) in enumerate(places):
                    a, w = (CT_AT[j], CT_W[j]) if window else (T_AT[j], T_W[j])
                    act.activation(pt_h[:, a:a + w], banks[b][:, o:o + w], ACT.Copy).then_inc(sm.turned_hi, 1)

            def qk_hi(sm, dst):
                wait(act, tile_read, at.t)
                act.activation(dst, af[0], ACT.Copy).then_inc(sm.qk_hi, 1)

            def out_hi(pair):
                hold(act, (att.o, pair * 2 + 2))
                act.activation(ao_h[pair.b] if not pair.a else arena_r[:, bass.ds((pair * S + 15 * S).val(), S)],
                               pair_tile(pair), ACT.Copy).then_inc(xh_ready, 1)

            def att_step(s, head_par, pair_par, unit_dst=None, late=True, early=True, pair=None, half=False,
                         ended=None):
                if late:
                    if head_par == 0:
                        hold(act, (att.pv, s - 1))
                        act.activation(vs_h, pair_tile(pair), ACT.Copy).then_inc(stage_hi, 1)
                    turned_his(att, s - 1)
                if unit_dst is not None:
                    split()
                    at.step()
                if half:
                    split()
                    at.step(2, 2)
                if early:
                    exps(att, s, 1 - head_par)
                if unit_dst is not None:
                    qk_hi(att, unit_dst)
                if ended is not None:
                    out_hi(ended)
                if late:
                    lo = HEAD * head_par
                    hold(act, (att.pv, s))
                    act.activation(pair_tile(pair, lo, lo + HEAD), banks[7][lo:lo + HEAD, :], ACT.Copy).then_inc(att.o, 1)

            root(2)
            keep_rms(2)
            split()
            at.step()
            qk_hi(att, ah[0][0])
            split()
            at.step()
            qk_hi(att, ah[0][1])
            for c in range(2):
                for kk in range(4):
                    split()
                    at.step(1, 0)
                wait(act, products_done, at.pe)
                for t in range(TT):
                    act.activation(vf[:, 4 * c:4 * c + 4, t, :],
                                   banks[4 + t][:, :].rearrange("p (a d) -> p a d", a=4), ACT.Copy,
                                   scale=rcol[:, t:t + 1]).then_inc(att_v, 1)
            att_step(Lin(-1), 0, 0, ah[1][0], late=False, early=False)
            att_step(Lin(0), 1, 0, ah[1][1], late=False)
            for j in range(4):
                att_step(Lin(1 + j), j % 2, None, ah[(j // 2) % 2][j % 2], pair=Lin(j // 2))
            with act.Fori(0, 2) as i:
                at.enter(i, 4, 4, 4)
                for j in range(4):
                    att_step(Lin(5 + j, 4, i), j % 2, None, ah[(j // 2) % 2][j % 2], pair=Lin(2 + j // 2, 2, i),
                             ended=Lin(j // 2, 2, i) if j % 2 else None)
                at.leave(2)
            for s in range(13, 17):
                att_step(Lin(s), (s + 1) % 2, None, late=True, early=s < 16, pair=Lin((s - 1) // 2), half=True,
                         ended=Lin(s - 9) if s < 16 else None)
            out_hi(Lin(7))
            last_tiles(4, 3, C_MLP1, 2)
            mlp(3, 32)
            act.wait_ge(gains_made, 1)
            last_tiles(5, BOTH, C_BOTH, 1)

            root(BOTH)
            keep_rms(BOTH)
            split()
            at.step()
            qk_hi(hyb, ah[0][0])
            split()
            at.step()
            qk_hi(hyb, ah[0][1])
            for kk in range(4):
                split()
                at.step(1, 0)
            wait(act, products_done, at.pe)
            for t in range(TT):
                act.activation(hv_h[t], banks[4 + t][:, :], ACT.Copy, scale=rcol[:, t:t + 1]).then_inc(hyb_vh, 1)
            act.activation(wf_hi[:, :, :], wf_raw[:, :, :], ACT.Copy).then_inc(wf_h, 1)
            split()
            at.step()
            act.wait_ge(hc_turned, 1)
            act.activation(hc_h, banks[3][:, :], ACT.Copy).then_inc(hyb_vh, 1)
            for s in range(-1, 17):
                if s >= 1:
                    turned_his(hyb, Lin(s - 1), s - 1 >= 8)
                if s in HYB_UNITS or s in GATE_STEPS:
                    split()
                    at.step()
                if 0 <= s < 16:
                    if s >= 8:
                        par = s % 2
                        act.wait_ge(hyb.negmax, s + 1)
                        act.activation(es[par], nm[par], ACT.Exp, bias=sink_b[:, SINK_OF[s - 8]:SINK_OF[s - 8] + 1])\
                            .then_inc(sink_exp, 1)
                    exps(hyb, Lin(s), s % 2, s >= 8)
                if s in HYB_UNITS:
                    n, dst = HYB_UNITS[s]
                    qk_hi(hyb, ah[dst[0]][dst[1]])
                if s == -1:
                    act.wait_ge(f_step, 2)
                    act.activation(fe, fn, ACT.Exp).then_inc(f_act, 1)
                if s == 0:
                    act.wait_ge(f_step, 3)
                    act.activation(fn, fe, ACT.Ln).then_inc(f_act, 1)
                    act.wait_ge(cum_done, 1)
                    act.activation(cum_sb, banks[5][0:4, :], ACT.Copy, scale=-1.0).then_inc(cum_row, 1)
                if s >= 1:
                    hd = s - 1
                    lo = HEAD * (hd % 2)
                    act.wait_ge(hyb.pv, s)
                    act.activation(of[hd // 2][lo:lo + HEAD, :], banks[7][lo:lo + HEAD, :], ACT.Copy)\
                        .then_inc(hyb.o, 1)
                if 4 <= s + 1 < 8:
                    act.wait_ge(cum_bc, s + 1 - 3)
                    act.activation(bias[(s + 1) % 2], banks[5][:, :], ACT.Copy).then_inc(cum_bias, 1)
            act.wait_ge(hyb.o, 16)

            def merged_hi(c):
                wait(act, merged, c + 1)
                act.activation(mg_h[c.b] if not c.a else arena_r[:, bass.ds((c * S + 16 * S).val(), S)],
                               mf_at(c), ACT.Copy).then_inc(xh_ready, 1)

            split()
            at.step(1, 0)
            for j in range(KT):
                act.activation(oh[j], of[j], ACT.Copy).then_inc(o_hi, 1)
            for c in range(2):
                split()
                at.step(1, 0)
                wait(act, tile_read, at.t)
                for g in range(3):
                    act.activation(gate_0[3 * c + g], gate_0[3 * c + g], ACT.Sigmoid).then_inc(gate_sig, 1)
            wait(act, gate_read, 3)
            for g in range(3):
                act.activation(gf[g], gf[g], ACT.Sigmoid).then_inc(gate_sig, 1)
            for c in range(3):
                split()
                at.step(1, 0)
                if c:
                    merged_hi(Lin(c - 1))

            with act.Fori(0, 5) as i:
                at.enter(i, 4, 4, 0)
                c = Lin(3, 1, i)
                for g in range(3):
                    split()
                    at.step(1, 0)
                    wait(act, gate_read, (c - 2) * 3 + (g + 1))
                    act.activation(gf[g], gf[g], ACT.Sigmoid).then_inc(gate_sig, 1)
                    if g == 0:
                        merged_hi(c - 1)
                split()
                at.step(1, 0)
                at.leave(5)
            merged_hi(Lin(KT - 1))
            last_tiles(7, 5, C_LN2, 1)
            root(5)
            keep_rms(5)

            def his(pair):
                tile = (pair - 1).fold(12)
                hold(act, (s_ready, pair + 1))
                act.activation(sh_all[:, bass.ds(tile.val(), 1), :].rearrange("p a n -> p (a n)"), sf[pair.b % 2],
                               ACT.Copy).then_inc(s_hi, 1)

            def glu_pair(pair, first=False):
                for n in range(2):
                    split()
                    at.step()
                    hold(act, (tile_read, at.t))
                    k = pair + n * PAIRS
                    act.activation(cy[2 * (pair.b % 2) + n], cz[2 * (pair.b % 2) + n][:, 2:S + 2], ACT.Identity,
                                   scale=col(k + (C_CW + 2 * 2 * PAIRS)), bias=col(k + C_CB)).then_inc(conv_0, 1)
                if not first:
                    his(pair - 1)
                y = cy[2 * (pair.b % 2)]
                wait(act, conv_2, pair * 2 + 1)
                act.activation(y, y, ACT.Silu).then_inc(silu_done, 1)

            glu_pair(Lin(0), True)
            glu_pair(Lin(1))
            for g in range(3):
                with act.Fori(0, 3) as i:
                    at.enter(i, 4, 4, 4)
                    for j in range(2):
                        glu_pair(Lin(2 + 6 * g + j, 2, i))
                    at.leave(3)
                if g < 2:
                    for j in range(KT):
                        split()
                        at.step()
            glu_pair(Lin(PAIRS - 2))
            glu_pair(Lin(PAIRS - 1))
            his(Lin(PAIRS - 1))
            for j in range(KT):
                split()
                at.step()
            last_tiles(None, 6, None, 1, final=True)
            root(6)

        @block.vector
        def _(dve):
            hold = holder(xh_ready)
            at = Place()

            next_split_made = [False]

            def split(ahead=LEAD):
                if next_split_made[0]:
                    next_split_made[0] = False
                    return
                u = at.u + ahead
                if u.a == 0 and u.b >= N_UNITS:
                    return
                wait(dve, hi_ready, u + 1)
                s = u % RING
                dve.tensor_tensor(w_lo[:, s, :], raw[:, s, :], f32(w_hi[:, s, :]), ALU.subtract).then_inc(lo_ready, 1)

            def x_lo_of(q, j, gain):
                wait(dve, xh_ready, 8 * q + j + 1)
                g = gains_2[:, j:j + 1] if gain == C_BOTH else col(gain + j)
                dve.scalar_tensor_tensor(x_lo[:, j, :], h[:, j, :], g, f32(x_hi[:, j, :]),
                                         ALU.mult, ALU.subtract).then_inc(xl_ready, 1)

            def rms(n):
                if 0 < n < NORMS - 1:
                    split()
                    next_split_made[0] = True
                if n == BOTH:
                    both_rms()
                    return
                wait(dve, stat_done, 2 * n + 1)
                dve.tensor_scalar(ms, banks[2][:, 0:4], 1.0 / D, EPS, ALU.mult, ALU.add).then_inc(ms_ready, 1)
                wait(dve, sd_ready, n + 1)
                dve.reciprocal(rcol, sd).then_inc(rcol_ready, 1)
                wait(dve, rcol_ready, n + 1)
                make_diag(rcol).then_inc(diag_ready, 1)

            def both_rms():
                wait(dve, stat_done, 2 * BOTH + 1)
                dve.tensor_scalar(ms_2[:, 4:8], banks[2][:, 0:4], 1.0 / D, EPS, ALU.mult, ALU.add).then_inc(ms_part, 1)
                dve.tensor_scalar(m2, banks[2][:, 4:8], 1.0 / D, None, ALU.mult).then_inc(ms_part, 1)
                wait(dve, ms_part, 2)
                dve.scalar_tensor_tensor(ms_2[:, 0:4], ms_2[:, 4:8], EPS, m2, ALU.mult, ALU.add).then_inc(ms_ready, 1)
                wait(dve, sd_ready, BOTH + 1)
                dve.reciprocal(rcol, sd_2[:, 0:4]).then_inc(rcol_ready, 1)
                dve.reciprocal(r_first, sd_2[:, 4:8]).then_inc(r_first_ready, 1)
                wait(dve, rcol_ready, BOTH + 1)
                make_diag(rcol).then_inc(diag_ready, 1)

            def make_diag(r):
                return dve.tensor_tensor(diag[:, :, :], ident[:, :].unsqueeze(1).broadcast_to([P, TT, P]),
                                         r.unsqueeze(2).broadcast_to([P, TT, P]), ALU.mult)

            def scaled(dst):
                wait(dve, products_done, at.pe)
                return dve.tensor_tensor(dst, banks[(at.t - 1) % 2][:, :], rbc[:, :], ALU.mult)

            def add_tile(j):
                wait(dve, products_done, at.pe)
                dve.tensor_tensor(h[:, j, :], banks[(at.t - 1) % 2][:, :], h[:, j, :], ALU.add).then_inc(tile_read, 1)

            dve.memset(ones[:, :], 1.0).then_inc(consts_made, 1)
            dve.wait_ge(cols_landed, 16)
            dve.tensor_tensor(gains_2, colv[:, C_FIN:C_FIN + KT], colv[:, C_LN1:C_LN1 + KT], ALU.mult)\
                .then_inc(gains_made, 1)
            for j in range(KT):
                dve.wait_ge(x_landed[j], 16)
                x_lo_of(0, j, C_MIX0)
                if j in (0, 4, 6):
                    split(max(0, j // 2 - 1))
            dve.wait_ge(strip_made, 1)
            dve.tensor_copy(strip_sb[:, 0:512], banks[6][0:12, 0:512])
            dve.tensor_copy(strip_sb[:, 512:640], banks[7][0:12, 0:128]).then_inc(strip_copied, 1)

            def y_of(hd):
                wait(dve, gn_done, hd * 3 + 3)

                def gated(c):
                    if c == 0:
                        wait(dve, gate_ready, hd * 4 + 4)
                    wait(dve, y_scaled, hd * 4 + (c + 1))
                    dve.tensor_tensor(oc[c], oc[c], sg[c], ALU.mult).then_inc(y_ready, 1)

                for c in range(4):
                    dve.scalar_tensor_tensor(oc[c], oc[c], col(hd * 4 + (C_GN + c)), banks[2][:, :],
                                             ALU.mult, ALU.mult).then_inc(y_scaled, 1)
                    if c:
                        gated(c - 1)
                gated(3)

            def rotate(hd, x, part, between=None):
                wait(dve, products_done, at.pe)
                src = banks[(at.t - 1) % 2][:, :]
                if part == 0:
                    dve.tensor_tensor(rt[0], src, cosr, ALU.mult)
                    dve.tensor_tensor(rt[1], src, sinr, ALU.mult).then_inc(tile_read, 1)
                    return
                dve.tensor_tensor(rt[2], src, sinr, ALU.mult)
                dve.tensor_tensor(rt[3], src, cosr, ALU.mult).then_inc(tile_read, 1)
                wait(dve, rope_lo, hd * 4 + 2 * x)
                wait(dve, tile_read, at.t)
                dve.tensor_tensor(qkf[0], rt[0], rt[2], ALU.subtract).then_inc(rope_ready, 1)
                dve.tensor_tensor(qkf[1], rt[1], rt[3], ALU.add).then_inc(rope_ready, 1)

            def ret_head(hd, first):
                split()
                if first:
                    dve.wait_ge(squares_landed, 16)
                    rms(0)
                    dve.wait_ge(rbc_ready, 1)
                    dve.wait_ge(rope_landed, 32)
                    dve.tensor_tensor(cosr, cosr, rbc[:, :], ALU.mult)
                    dve.tensor_tensor(sinr, sinr, rbc[:, :], ALU.mult).then_inc(rope_tables, 1)
                    dve.wait_ge(rope_tables, 1)
                    dve.wait_ge(masks_ready, 1)
                at.step()
                wait(dve, ret_p_lo, hd * 4)
                rotate(hd, 0, 0)
                split()
                if not first:
                    y_of(hd - 1)
                at.step()
                rotate(hd, 0, 1)
                split()
                at.step()
                rotate(hd, 1, 0)
                split()
                at.step()
                rotate(hd, 1, 1)
                for kk in range(4):
                    split()
                    at.step(1, 0)
                for t in range(TT):
                    wait(dve, v_hi, hd * 4 + (t + 1))
                    dve.scalar_tensor_tensor(rv_l[t], banks[4 + t][:, :], rcol[:, t:t + 1], f32(rv_h[t]),
                                             ALU.mult, ALU.subtract).then_inc(v_lo, 1)
                if not first:
                    for n in range(4):
                        split()
                        for c in range(2):
                            at.pe, at.t = at.pe + 1, at.t + 1
                            add_tile(2 * n + c)
                        at.u = at.u + 1
                wait(dve, decay_landed, (hd + 1) * 16)
                for j, (b, o) in enumerate([(2, 0), (3, 0), (4, 0), (4, 256)]):
                    wait(dve, ret_scores, hd * 4 + (j + 1 if j != 2 else 4))
                    dve.tensor_tensor(pf_ret[:, T_AT[j]:T_AT[j] + T_W[j]], banks[b][:, o:o + T_W[j]],
                                      decay[:, 0:T_W[j]], ALU.mult).then_inc(ret_p, 1)
                for c in range(4):
                    split()
                    if c == 2:
                        wait(dve, gn_done, hd * 3 + 1)
                        for e in range(4):
                            dve.scalar_tensor_tensor(oc[e], banks[2][:, :], -1.0 / RV, oc[e],
                                                     ALU.mult, ALU.add).then_inc(gn_centred, 1)
                    if c == 3:
                        wait(dve, gn_done, hd * 3 + 2)
                        dve.tensor_scalar(gn_ms, banks[3][:, 0:4], 1.0 / RV, EPS, ALU.mult, ALU.add)\
                            .then_inc(gn_ms_r, 1)
                        wait(dve, gn_sd_r, hd + 1)
                        dve.reciprocal(gn_r, gn_sd).then_inc(gn_r_r, 1)
                        wait(dve, gn_r_r, hd + 1)
                        make_diag(gn_r).then_inc(gn_diag, 1)
                    at.step()
                    scaled(sg[c]).then_inc(tile_read, 1)

            ret_head(Lin(0), True)
            with dve.Fori(0, RH - 1) as i:
                at.enter(i, 16, 20, 16)
                ret_head(Lin(1, 1, i), False)
                at.leave(RH - 1)
            split()
            next_split_made[0] = True
            y_of(Lin(RH - 1))

            def last_tiles(q, gain, per_unit):
                if q is None:
                    for j in range(KT):
                        split()
                        at.step()
                        add_tile(j)
                    return
                for j in range(KT):
                    if j % per_unit == 0:
                        split()
                        at.u = at.u + 1
                    at.pe, at.t = at.pe + 1, at.t + 1
                    add_tile(j)
                    if j:
                        x_lo_of(q, j - 1, gain)
                x_lo_of(q, KT - 1, gain)

            last_tiles(1, C_MLP0, 2)

            def mlp_up(base):
                for j in range(KT):
                    split()
                    at.step()
                    scaled(zf[j % 2]).then_inc(tile_read, 1)
                    wait(dve, tile_read, at.t)
                    dve.scalar_tensor_tensor(uf[j % 2], zf[j % 2], 0.0, zf[j % 2], ALU.max, ALU.mult)\
                        .then_inc(u_ready, 1)
                    wait(dve, u_hi, lin(base) + (j + 1))
                    dve.tensor_tensor(ul[j], uf[j % 2], f32(uh[j]), ALU.subtract).then_inc(u_lo, 1)

            def mlp(n, base):
                rms(n)
                dve.wait_ge(rbc_ready, n + 1)
                mlp_up(base)
                with dve.Fori(0, 3) as i:
                    at.enter(i, 16, 16, 16)
                    for j in range(KT):
                        split()
                        at.step()
                        add_tile(j)
                    mlp_up(Lin(base + 8, 8, i))
                    at.leave(3)

            mlp(1, 0)
            last_tiles(2, C_MIX1, 1)

            def maxima(sm, hd, par, n_bias, kind, sink=None):
                hold(dve, (sm.scores, hd + 1), *([n_bias] if n_bias is not None else []))
                window = kind == "window"
                places = [(2, 0), (2, 128), (3, 0), (3, 256)] if window else [(2, 0), (4, 0), (2, 128), (3, 0)]
                for t, (b, o) in enumerate(places):
                    a, w = (CP_AT[t], CP_W[t]) if window else (P_AT[t], P_W[t])
                    if window:
                        bt = bias[par][:, 256 - w:256]
                    elif kind == "key":
                        bt = bias[par][:, 0:w]
                    else:
                        bt = bias[par][:, S - w:S]
                    dve.tensor_tensor_reduce(pf[par][:, a:a + w], banks[b][:, o:o + w], bt, 1.0, LOWEST,
                                             ALU.add, ALU.max, mx[par][:, t:t + 1]).then_inc(sm.biased, 1)
                wait(dve, sm.biased, hd * 4 + 4)
                if sink is None:
                    dve.tensor_scalar(nm[par], mx[par], -1.0, None, ALU.mult).then_inc(sm.negmax, 1)
                else:
                    dve.tensor_scalar(nm[par], mx[par], -1.0, nsink[:, sink:sink + 1], ALU.mult, ALU.min)\
                        .then_inc(sm.negmax, 1)

            def turned_los(sm, hd, window=False):
                places = [(5, 0), (5, 256), (6, 0), (6, 256)] if window else [(5, 0), (6, 0), (7, 0), (6, 384)]
                for j, (b, o) in enumerate(places):
                    a, w = (CT_AT[j], CT_W[j]) if window else (T_AT[j], T_W[j])
                    wait(dve, sm.turned_hi, hd * 4 + ((2, 2, 4, 4) if window else (1, 4, 4, 4))[j])
                    dve.tensor_tensor(pt_l[:, a:a + w], banks[b][:, o:o + w], f32(pt_h[:, a:a + w]),
                                      ALU.subtract).then_inc(sm.turned_lo, 1)

            def inverse(sm, hd, par):
                wait(dve, sm.exp, hd * 4 + 4)
                dve.reciprocal(rinv[par], sums[par]).then_inc(sm.rinv, 1)

            def qk_tile(sm, n, scale, dst):
                wait(dve, sm.qk_lo, n)
                wait(dve, products_done, at.pe)
                dve.scalar_tensor_tensor(af[0], banks[(at.t - 1) % 2][:, :], scale, rbc[:, :], ALU.mult, ALU.mult)\
                    .then_inc(tile_read, 1)
                wait(dve, sm.qk_hi, lin(n) + 1)
                dve.tensor_tensor(dst[1], af[0], f32(dst[0]), ALU.subtract).then_inc(sm.qk_lo, 1)

            def out_lo(pair):
                wait(dve, xh_ready, pair + (24 + 1))
                hi, lo = (ao_h[pair.b], ao_l[pair.b]) if not pair.a else (
                    arena_r[:, bass.ds((pair * S + n * S).val(), S)] for n in (15, 23))
                dve.tensor_tensor(lo, pair_tile(pair), f32(hi), ALU.subtract).then_inc(xl_ready, 1)

            def att_step(s, head_par, unit=None, late=True, early=True, pair=None, half=None, ended=None):
                if early:
                    hd = s
                    maxima(att, hd, 1 - head_par, (bias_masked, hd + 1), "rel")
                if late:
                    if head_par == 0:
                        wait(dve, stage_hi, (s + 1) // 2)
                        dve.tensor_tensor(vs_l, pair_tile(pair), f32(vs_h), ALU.subtract).then_inc(stage_lo, 1)
                    turned_los(att, s - 1)
                if unit is not None or half is not None:
                    split()
                if early:
                    inverse(att, s, 1 - head_par)
                if half is not None:
                    at.u = at.u + 1
                    for c in range(2):
                        at.pe, at.t = at.pe + 1, at.t + 1
                        add_tile(2 * half + c)
                if unit is not None:
                    at.step()
                    qk_tile(att, s + 3, SCALE if unit[1] == 0 else 1.0, (ah[unit[0]][unit[1]], al[unit[0]][unit[1]]))
                if ended is not None:
                    out_lo(ended)

            rms(2)
            dve.wait_ge(rbc_ready, 3)
            for n in range(2):
                split()
                at.step()
                qk_tile(att, n, (SCALE, 1.0)[n], (ah[0][n], al[0][n]))
            for _ in range(8):
                split()
                at.step(1, 0)
            att_step(Lin(-1), 0, (1, 0), late=False, early=False)
            att_step(Lin(0), 1, (1, 1), late=False)
            for j in range(4):
                att_step(Lin(1 + j), j % 2, ((j // 2) % 2, j % 2), pair=Lin(j // 2))
            with dve.Fori(0, 2) as i:
                at.enter(i, 4, 4, 4)
                for j in range(4):
                    att_step(Lin(5 + j, 4, i), j % 2, ((j // 2) % 2, j % 2), pair=Lin(2 + j // 2, 2, i),
                             ended=Lin(j // 2, 2, i) if j % 2 else None)
                at.leave(2)
            for s in range(13, 17):
                att_step(Lin(s), (s + 1) % 2, None, early=s < 16, pair=Lin((s - 1) // 2), half=s - 13,
                         ended=Lin(s - 9) if s < 16 else None)
            out_lo(Lin(7))
            last_tiles(4, C_MLP1, 2)
            mlp(3, 32)
            last_tiles(5, C_BOTH, 1)

            rms(BOTH)
            dve.wait_ge(rbc_ready, BOTH + 1)
            dve.wait_ge(r_first_ready, 1)
            make_diag(r_first).then_inc(first_diag, 1)
            for n in range(2):
                split()
                at.step()
                qk_tile(hyb, n, (SCALE, 1.0)[n], (ah[0][n], al[0][n]))
            for kk in range(4):
                split()
                at.step(1, 0)
                if kk == 1:
                    dve.wait_ge(first_spread, 1)
                if kk:
                    for j in range(3 * kk - 3, min(3 * kk, KT)):
                        dve.scalar_tensor_tensor(h[:, j, :], h[:, j, :], col(C_FIN + j), banks[3][:, :],
                                                 ALU.mult, ALU.mult).then_inc(h_normed, 1)
            for t in range(TT):
                wait(dve, hyb_vh, t + 1)
                dve.scalar_tensor_tensor(hv_l[t], banks[4 + t][:, :], rcol[:, t:t + 1], f32(hv_h[t]),
                                         ALU.mult, ALU.subtract).then_inc(hyb_vl, 1)
            dve.wait_ge(wf_h, 1)
            dve.tensor_tensor(wf_lo[:, :, :], wf_raw[:, :, :], f32(wf_hi[:, :, :]), ALU.subtract).then_inc(wf_l, 1)
            dve.wait_ge(small_in, 48)
            dve.tensor_scalar(nsink, sink_b, -1.0, None, ALU.mult).then_inc(sink_ready, 1)
            split()
            at.step()
            scaled(hc_f).then_inc(tile_read, 1)
            dve.wait_ge(f_done, 1)
            dve.tensor_tensor(f_row, banks[2][0:4, :], rbc[0:4, :], ALU.mult).then_inc(f_row_ready, 1)
            dve.wait_ge(hyb_vh, 5)
            dve.tensor_tensor(hc_l, banks[3][:, :], f32(hc_h), ALU.subtract).then_inc(hyb_vl, 1)
            for s in range(-1, 17):
                if 0 <= s < 16:
                    kind = "rel" if s < 4 else "key" if s < 8 else "window"
                    if 4 <= s < 8:
                        dve.wait_ge(cum_bias, s - 3)
                    if s == 8:
                        dve.wait_ge(sink_ready, 1)
                    maxima(hyb, Lin(s), s % 2, (hyb.bias[s % 2], BIAS_COUNT[s]) if BIAS_COUNT[s] else None, kind,
                           None if s < 8 else SINK_OF[s - 8])
                if s == 0:
                    dve.wait_ge(f_act, 1)
                    dve.tensor_scalar(fe, fe, 1.0, None, ALU.add).then_inc(f_step, 1)
                    dve.wait_ge(f_step, 2)
                    dve.tensor_scalar(fl, fl, 0.0, None, ALU.min).then_inc(f_step, 1)
                if s >= 1:
                    turned_los(hyb, Lin(s - 1), s - 1 >= 8)
                if s in HYB_UNITS or s in GATE_STEPS:
                    split()
                if 0 <= s < 8:
                    inverse(hyb, Lin(s), s % 2)
                elif 8 <= s < 16:
                    dve.wait_ge(hyb.exp, 4 * s + 4)
                    dve.wait_ge(sink_exp, s - 7)
                    dve.tensor_tensor(sums2[s % 2], sums[s % 2], es[s % 2], ALU.add).then_inc(sink_sum, 1)
                    dve.wait_ge(sink_sum, s - 7)
                    dve.reciprocal(rinv[s % 2], sums2[s % 2]).then_inc(hyb.rinv, 1)
                if s in HYB_UNITS:
                    n, (a, b) = HYB_UNITS[s]
                    at.step()
                    qk_tile(hyb, n, SCALE if b == 0 else 1.0, (ah[a][b], al[a][b]))
                if s in GATE_STEPS:
                    at.step()
                    scaled(gate_0[GATE_STEPS[s]]).then_inc(tile_read, 1)
                if s == -1:
                    dve.wait_ge(f_done, 2)
                    dve.tensor_tensor(fl.rearrange("p (t a) -> p t a", t=TT),
                                      banks[6][:, 0:16].rearrange("p (t a) -> p t a", t=TT),
                                      fb_b.unsqueeze(1).broadcast_to([P, TT, 4]), ALU.add).then_inc(f_step, 1)
                    dve.wait_ge(f_step, 1)
                    dve.scalar_tensor_tensor(fn, fl, -1.0, fl, ALU.mult, ALU.min).then_inc(f_step, 1)
                if s == 0:
                    dve.wait_ge(f_act, 2)
                    dve.wait_ge(f_step, 4)
                    dve.tensor_tensor(flog, fl, fn, ALU.subtract).then_inc(f_step, 1)
            def merged_lo(c):
                wait(dve, xh_ready, c + (48 + 1))
                if c.a:
                    hi, lo = (arena_r[:, bass.ds((c * S + n * S).val(), S)] for n in (16, 24))
                else:
                    hi, lo = mg_h[c.b], mg_l[c.b]
                dve.tensor_tensor(lo, mf_at(c), f32(hi), ALU.subtract).then_inc(xl_ready, 1)

            def gates(c, between=None):
                for g, b in enumerate((0, 1, 5)):
                    split()
                    at.step(1, 0)
                    wait(dve, products_done, at.pe)
                    dve.tensor_tensor(gf[g], banks[b][:, :], rbc[:, :], ALU.mult).then_inc(gate_read, 1)
                    if between:
                        between(g)

            def branches(c, gate):
                split()
                at.step(1, 0)
                wait(dve, products_done, at.pe)
                wait(dve, merged, c)
                for g in range(3):
                    wait(dve, gate_sig, c * 3 + (g + 1))
                    dve.tensor_tensor(mt[g], banks[2 + g][:, :], gate[g], ALU.mult).then_inc(branch_read, 1)
                wait(dve, branch_read, c * 3 + 3)
                dve.tensor_tensor(mt[3], mt[0], mt[1], ALU.add).then_inc(merge_a, 1)
                wait(dve, merge_a, c + 1)
                dve.tensor_tensor(mf_at(c), mt[3], mt[2], ALU.add).then_inc(merged, 1)

            def o_los(g):
                for j in range(4 * g, min(4 * g + 4, KT)):
                    wait(dve, o_hi, j + 1)
                    dve.tensor_tensor(ol[j], of[j], f32(oh[j]), ALU.subtract).then_inc(o_lo, 1)

            gates(Lin(2), o_los)
            for c in range(3):
                branches(Lin(c), gate_0[3 * c:3 * c + 3] if c < 2 else gf)
                if c:
                    merged_lo(Lin(c - 1))
            with dve.Fori(0, 3) as i:
                at.enter(i, 4, 4, 0)
                c = Lin(3, 1, i)
                gates(c, lambda g: merged_lo(c - 1) if g == 1 else None)
                branches(c, gf)
                at.leave(3)
            for c in (6, 7):
                gates(Lin(c))
                branches(Lin(c), gf)
            for c in range(5, 8):
                merged_lo(Lin(c))
            last_tiles(7, C_LN2, 1)
            rms(5)
            dve.wait_ge(rbc_ready, 6)

            for n in range(4):
                m = dve.memset(cz[n][:, 0:2], 0.0)
            m.then_inc(pad_made, 1)
            dve.wait_ge(pad_made, 1)

            def taps(pair, n):
                par = pair.b % 2
                z, y, k = cz[2 * par + n], cy[2 * par + n], pair + n * PAIRS
                wait(dve, conv_0, pair * 2 + (n + 1))
                dve.scalar_tensor_tensor(y, z[:, 1:S + 1], col(k + (C_CW + 2 * PAIRS)), y, ALU.mult, ALU.add)\
                    .then_inc(conv_1, 1)
                wait(dve, conv_1, pair * 2 + (n + 1))
                dve.scalar_tensor_tensor(y, z[:, 0:S], col(k + C_CW), y, ALU.mult, ALU.add).then_inc(conv_2, 1)

            def product(pair):
                par = pair.b % 2
                wait(dve, silu_done, pair + 1)
                wait(dve, conv_2, pair * 2 + 2)
                dve.tensor_tensor(sf[par], cy[2 * par], cy[2 * par + 1], ALU.mult).then_inc(s_ready, 1)

            def los(pair):
                at_12 = bass.ds((pair - 1).fold(12).val(), 1)
                wait(dve, s_hi, pair + 1)
                dve.tensor_tensor(sl_all[:, at_12, :].rearrange("p a n -> p (a n)"), sf[pair.b % 2],
                                  f32(sh_all[:, at_12, :].rearrange("p a n -> p (a n)")), ALU.subtract)\
                    .then_inc(s_lo, 1)

            def glu_pair(pair, first=False):
                for n in range(2):
                    split()
                    at.step()
                    scaled(cz[2 * (pair.b % 2) + n][:, 2:S + 2]).then_inc(tile_read, 1)
                    if n == 0 and not first:
                        taps(pair - 1, 1)
                    if n == 1:
                        if not first:
                            product(pair - 1)
                        taps(pair, 0)
                        if not first:
                            los(pair - 1)

            glu_pair(Lin(0), True)
            glu_pair(Lin(1))
            for g in range(3):
                with dve.Fori(0, 3) as i:
                    at.enter(i, 4, 4, 4)
                    for j in range(2):
                        glu_pair(Lin(2 + 6 * g + j, 2, i))
                    at.leave(3)
                if g < 2:
                    for j in range(KT):
                        split()
                        at.step()
                        add_tile(j)
            glu_pair(Lin(PAIRS - 2))
            glu_pair(Lin(PAIRS - 1))
            taps(Lin(PAIRS - 1), 1)
            product(Lin(PAIRS - 1))
            los(Lin(PAIRS - 1))
            for j in range(KT):
                split()
                at.step()
                add_tile(j)
            last_tiles(None, None, 1)
            rms(6)
            dve.wait_ge(stat_done, 2 * NORMS)
            for j in range(KT):
                dve.scalar_tensor_tensor(h[:, j, :], h[:, j, :], col(C_LNF + j), banks[3][:, :], ALU.mult, ALU.mult)\
                    .then_inc(out_ready, 1)

        @block.gpsimd
        def _(pool):
            hold = holder(xh_ready)
            pool.dma_start(onehot_sb, c_onehot).then_inc(strip_in, 16)
            pool.dma_start(rel_sb[0:BUCKETS, :], rel_2).then_inc(strip_in, 16)
            pool.dma_start(rel_sb[BUCKETS:BUCKETS + 2, :], c_masked).then_inc(strip_in, 16)
            pool.dma_start(ident[:, :], c_sq[0]).then_inc(squares_landed, 16)
            pool.dma_start(masks_sb, c_sq.rearrange("m p n -> p m n")).then_inc(masks_landed, 16)
            pool.dma_start(decay, c_decay[0:P, :]).then_inc(decay_landed, 16)
            pool.dma_start(wf_raw[:, :, :], wf).then_inc(small_in, 16)
            pool.dma_start(fb_b, f_bias.partition_broadcast(P)).then_inc(small_in, 16)
            pool.dma_start(sink_b, sinks.partition_broadcast(P)).then_inc(small_in, 16)

            def sum_squares(n):
                wait(pool, sq_ready, 8 * n + 2)
                pool.tensor_tensor(acc[:, :], sq[:, 0, :], sq[:, 1, :], ALU.add).then_inc(acc_sum, 1)
                for k in range(1, 6):
                    wait(pool, acc_sum, 6 * n + k)
                    wait(pool, sq_ready, 8 * n + k + 2)
                    pool.tensor_tensor(acc[:, :], acc[:, :], sq[:, (k + 1) % 4, :], ALU.add).then_inc(acc_sum, 1)

            def sum_both():
                for k in range(7):
                    if k < 6:
                        if k:
                            wait(pool, acc_sum, 6 * BOTH + k)
                        wait(pool, sq_ready, 8 * BOTH + k + 2)
                        pool.tensor_tensor(acc[:, :], acc[:, :] if k else sq[:, 0, :], sq[:, (k + 1) % 4, :], ALU.add)\
                            .then_inc(acc_sum, 1)
                    wait(pool, sum2, k)
                    wait(pool, sq2_ready, k + 2)
                    pool.tensor_tensor(acc2, acc2 if k else sq2[0], sq2[(k + 1) % 4], ALU.add).then_inc(sum2, 1)

            sum_squares(0)
            pool.wait_ge(strip_copied, 1)
            pool.dma_start(strips, strip_sb.unsqueeze(1).broadcast_to([12, P, STRIP])).then_inc(strip_saved, 16)

            def y_los(hd):
                for c in range(4):
                    wait(pool, y_hi, hd * 4 + (c + 1))
                    pool.tensor_tensor(ry_l[c], oc[c], f32(ry_h[c]), ALU.subtract).then_inc(y_lo, 1)

            def ret_head(hd, first):
                if not first:
                    wait(pool, ret_p, hd * 4)
                    pool.dma_start(decay, c_decay[bass.ds((hd * P).val(), P), :]).then_inc(decay_landed, 16)
                    y_los(hd - 1)
                for n in range(4):
                    wait(pool, rope_hi, hd * 4 + (n + 1))
                    pool.tensor_tensor(rqk_l[n], qkf[n % 2], f32(rqk_h[n]), ALU.subtract).then_inc(rope_lo, 1)
                for j in range(TT):
                    a, w = T_AT[j], T_W[j]
                    wait(pool, ret_p_hi, hd * 4 + (j + 1))
                    pool.tensor_tensor(rp_l[:, a:a + w], pf_ret[:, a:a + w], f32(rp_h[:, a:a + w]), ALU.subtract)\
                        .then_inc(ret_p_lo, 1)
                for k, (src, ready) in enumerate(((oc, ret_o), ([sq[:, c, :] for c in range(4)], gn_sq))):
                    wait(pool, ready, hd * 4 + 2)
                    pool.tensor_tensor(acc[:, :], src[0], src[1], ALU.add).then_inc(gn_sum, 1)
                    for c in (2, 3):
                        wait(pool, ready, hd * 4 + (c + 1))
                        wait(pool, gn_sum, hd * 6 + (3 * k + c - 1))
                        pool.tensor_tensor(acc[:, :], acc[:, :], src[c], ALU.add).then_inc(gn_sum, 1)

            ret_head(Lin(0), True)
            with pool.Fori(0, RH - 1) as i:
                ret_head(Lin(1, 1, i), False)
            y_los(Lin(RH - 1))
            sum_squares(1)
            sum_squares(2)

            def normalise(sm, hd, par, window=False):
                hold(pool, (sm.rinv, hd + 1))
                for t in range(TT):
                    a, w = (CP_AT[t], CP_W[t]) if window else (P_AT[t], P_W[t])
                    pool.tensor_scalar(pf[par][:, a:a + w], pf[par][:, a:a + w], rinv[par][:, t:t + 1], 1.0,
                                       ALU.mult, ALU.mult).then_inc(sm.probs, 1)

            def toeplitz(sm, hd, table, row, offset, w):
                wait(pool, sm.biased, 4 * (hd - 1) if hd >= 2 else 0)
                src = bass.AP(table.tensor, row * P * STRIP + offset + P - 1, [[STRIP - 1, P], [1, w]])
                pool.dma_start(bias[hd % 2][:, 0:w], src).then_inc(sm.bias[hd % 2], 16)

            def mask_chunks(hd):
                last = bias[hd % 2][:, S - P:S]
                pool.wait_ge(att.bias[hd % 2], 16 * (hd // 2 + 1))
                pool.tensor_tensor(last, last, f32(sqr[:, 1, :]), ALU.add).then_inc(bias_masked, 1)

            pool.wait_ge(masks_ready, 1)
            for hd in range(2):
                toeplitz(att, hd, rel_pad, hd, 0, S)
            mask_chunks(0)
            for hd in range(AH):
                if hd + 1 < AH:
                    mask_chunks(hd + 1)
                normalise(att, hd, hd % 2)
                if hd + 2 < AH:
                    toeplitz(att, hd + 2, rel_pad, hd + 2, 0, S)
            sum_squares(3)
            sum_both()
            pool.wait_ge(xl_ready, 32)
            pool.dma_start(tri_sb, c_tri).then_inc(tri_landed, 16)
            pool.dma_start(sel_sb, c_sel).then_inc(tri_landed, 16)
            pool.wait_ge(strip_saved, 16)

            def hyb_bias(hd):
                if hd < 4:
                    toeplitz(hyb, hd, strips, hd, 0, S)
                elif 8 <= hd < 16:
                    toeplitz(hyb, hd, strips, 4 + SINK_OF[hd - 8], 256, 2 * P)

            hyb_bias(0)
            hyb_bias(1)
            for hd in range(16):
                normalise(hyb, hd, hd % 2, hd >= 8)
                hyb_bias(hd + 2)
            sum_squares(5)
            sum_squares(6)


def rope_tables():
    half = RK // 2
    inv = np.exp(-np.log(10000.0) * np.arange(half) / half)
    ang = inv[:, None] * np.arange(S)[None, :]
    return np.stack([np.cos(ang), np.sin(ang)]).astype(np.float32)


def decay_tables():
    m, n = np.arange(P)[:, None], np.arange(S)[None, :]
    seen = m // CH <= n // CH
    gamma = 1.0 - 2.0 ** (-5.0 - np.arange(RH))
    tab = gamma[:, None, None] ** np.abs(n - m) * RK ** -0.5 * seen
    return tab.reshape(RH * P, S).astype(np.float32)


def square_tables():
    q, k = np.arange(P)[:, None], np.arange(P)[None, :]
    masks = [(q < CH) & (k >= CH), k > q]
    return np.stack([np.eye(P)] + [np.where(x, NEG, 0.0) for x in masks]).astype(np.float32)


def bucket_table():
    f = np.float32
    ahead = 511 - np.arange(STRIP)
    dist = np.maximum(ahead, 0)
    exact = BUCKETS // 2
    d = np.maximum(dist.astype(f), f(1))
    large = exact + (np.log(d / f(exact)) / f(np.log(MAX_DISTANCE / exact)) * f(BUCKETS - exact)).astype(np.int32)
    bucket = np.where(dist < exact, dist, np.minimum(large, BUCKETS - 1))
    onehot = np.arange(BUCKETS)[:, None] == bucket[None, :]
    masks = np.where([ahead < 0, ahead >= WINDOW], NEG, 0.0)
    return np.concatenate([onehot, masks]).astype(np.float32)


def features(w, c, k=KT):
    return w[:, c].reshape(k, P, P).transpose(1, 0, 2).reshape(P, k * P)


def units(a):
    out = []

    def tile(w, at):
        u = features(w, slice(at, at + P), w.shape[0] // P)
        out.append(np.pad(u, ((0, 0), (0, UNIT - u.shape[1]))))

    def tokens(w, at):
        for kk in range(4):
            out.append(w[kk * 256:(kk + 1) * 256, at:at + S].reshape(2, P, S).transpose(1, 0, 2).reshape(P, UNIT))

    def halves(w):
        for c in range(4):
            part = w[:, c * 256:(c + 1) * 256].reshape(4, P, 2, P)
            out.append(part.transpose(1, 2, 0, 3).reshape(P, UNIT))

    def head_out(hd):
        halves(a["ret_w_out"][0][hd * RV:(hd + 1) * RV])

    def mlp(n):
        for g in range(4):
            for c in range(8):
                tile(a["mlp_w1"][n], g * D + c * P)
            for c in range(8):
                tile(a["mlp_w2"][n][g * D:(g + 1) * D], c * P)

    w = a["ret_w_in"][0]
    for hd in range(RH):
        for at in (hd * RK, hd * RK + P, D + hd * RK, D + hd * RK + P):
            tile(w, at)
        tokens(w, 2 * D + hd * RV)
        if hd:
            head_out(hd - 1)
        for c in range(4):
            tile(w, 4 * D + hd * RV + c * P)
    head_out(RH - 1)
    mlp(0)
    w = a["att_w_in"][0]
    tile(w, 0)
    tile(w, D)
    tokens(w, 2 * D)
    tokens(w, 2 * D + S)
    for p in range(1, 8):
        tile(w, p * P)
        tile(w, D + p * P)
    halves(a["att_w_out"][0][:512])
    halves(a["att_w_out"][0][512:])
    mlp(1)
    w = a["w_in_2"][0]
    qa, ka, va, qb, kb, vb, fb, qc, kc, vc, ga, gb, gc = np.cumsum(
        [0, 256, 256, 256, 256, 256, 256, 4, 512, 128, 128, D, D])
    pairs = [np.r_[qc + j * HEAD:qc + (j + 1) * HEAD, qc + (j + 4) * HEAD:qc + (j + 5) * HEAD] for j in range(4)]
    tile(w, qa)
    tile(w, ka)
    tokens(np.concatenate([w[:, va:va + 256], w[:, vb:vb + 256]], 1), 0)
    tile(w, vc)
    tile(w, qa + P)
    tile(w, ka + P)
    for n in range(2):
        tile(w, qb + n * P)
        tile(w, kb + n * P)
    tile(w[:, pairs[0]], 0)
    tile(w, kc)

    def gate(n):
        tile(w, (ga, gb, gc)[n % 3] + n // 3 * P)

    for j in range(1, 4):
        tile(w[:, pairs[j]], 0)
        gate(j - 1)
    for n in range(3, 9):
        gate(n)
    rows = np.concatenate([pair - qc for pair in pairs])
    branches = np.concatenate([a["w_pa_2"][0], a["w_pb_2"][0], a["w_pc_2"][0][rows]], 0)
    for c in range(8):
        if c > 2:
            for g in range(3):
                gate(3 * c + g)
        tile(branches, c * P)
    for c in range(8):
        tile(a["w_o_2"][0], c * P)

    def up(pairs):
        for c in pairs:
            tile(a["w_up_2"][0], c * P)
            tile(a["w_up_2"][0], FF2 + c * P)

    def down(g):
        done = sum(GROUPS[:g])
        for c in range(8):
            tile(a["w_down_2"][0][done * P:(done + GROUPS[g]) * P], c * P)

    up(range(8))
    down(0)
    up(range(8, 14))
    down(1)
    up(range(14, PAIRS))
    down(2)
    down(3)
    assert len(out) == N_UNITS
    return np.stack(out)


def columns(v):
    return np.asarray(v).reshape(-1, P).T


def kernel(**inputs):
    import concourse.bacc as bacc
    from concourse.bass_utils import run_bass_kernel_spmd

    a = {k: np.asarray(v) for k, v in inputs.items()}
    fb = 6 * 256
    arrays = {
        "stream": units(a),
        "x_t": a["x"][0].T,
        "cols": np.concatenate([columns(v) for v in (
            a["mix_norm_g"][0], a["mlp_norm_g"][0], a["mix_norm_g"][1], a["mlp_norm_g"][1], a["final_norm_g"],
            a["ln1_2"][0], a["ln2_2"][0], a["ln_f_2"], a["ret_gn_g"][0],
            a["conv_w_2"][0].reshape(-1), a["conv_b_2"][0])], 1),
        "wf": a["w_in_2"][0][:, fb:fb + 4].reshape(KT, P, 4).transpose(1, 0, 2),
        "f_bias": a["b_f_2"][0],
        "sinks": a["sinks_2"][0],
        "rel_pad": np.repeat(np.pad(a["att_rel_bias"][0], (
            (0, 0), (S - 1 - REL_MAX, STRIP - REL_TABLE - (S - 1 - REL_MAX))), mode="edge")[:, None], P, axis=1),
        "rel_2": a["rel_bias_2"],
        "c_rope": rope_tables(),
        "c_decay": decay_tables(),
        "c_sq": square_tables(),
        "c_tri": (np.arange(P)[:, None] <= np.arange(S)[None, :]).astype(np.float32),
        "c_sel": np.repeat(np.eye(4), P, axis=1).astype(np.float32),
        "c_onehot": bucket_table(),
        "c_masked": np.stack([np.ones(12), np.arange(12) >= 4]).astype(np.float32),
    }
    nc = bacc.Bacc("TRN2", target_bir_lowering=False, num_devices=1)
    feed, args = {}, []
    for name, v in arrays.items():
        v = np.ascontiguousarray(v)
        feed["in_" + name] = v
        args.append(nc.dram_tensor("in_" + name, v.shape, mybir.dt.from_np(v.dtype), kind="ExternalInput").ap())
    out = nc.dram_tensor("out_t", (D, S), F32, kind="ExternalOutput").ap()
    build(nc, *args, out)
    got = run_bass_kernel_spmd(nc, [feed], core_ids=[0]).results[0]["out_t"]
    return np.ascontiguousarray(got.T)[None]
```
